# Optimizing a Trainium2 kernel written in Bass

```python
import math
import jax, jax.numpy as jnp
from jax import lax
import numpy as np

D_MODEL = 2048
BATCH = 1
SEQ = 256
DEPTH = 1

HEAD_DIM = 128
N_HEAD_SLOTS = 8
DILATED_GROUPS = ((128, 1), (512, 4), (2048, 16))
N_GROUPS = len(DILATED_GROUPS)
ATTN_WIDTH = N_HEAD_SLOTS * HEAD_DIM
POOL_WINDOWS = (2, 4, 8, 16)
N_POOL_GROUPS = len(POOL_WINDOWS)
POOL_WIDTH = D_MODEL // 2
POOL_GROUP = POOL_WIDTH // N_POOL_GROUPS
N_BRANCHES = 2
SPLIT_SIZES = (N_GROUPS * ATTN_WIDTH,
               N_GROUPS * ATTN_WIDTH,
               N_GROUPS * ATTN_WIDTH,
               ATTN_WIDTH,
               POOL_WIDTH,
               POOL_WIDTH,
               N_BRANCHES * D_MODEL)
IN_WIDTH = sum(SPLIT_SIZES)
DEEPNORM_ALPHA = (2.0 * DEPTH) ** 0.25
DEEPNORM_BETA = (8.0 * DEPTH) ** -0.25
LN_EPS = 1e-5
NEG_INF = -1e30

kernel_name = "hybrid_dilated_attn_pool_gated_deepnorm"

def layer_norm(x, gamma, beta):
    xf = x.astype(jnp.float32)
    mu = jnp.mean(xf, axis=-1, keepdims=True)
    var = jnp.mean(jnp.square(xf - mu), axis=-1, keepdims=True)
    y = (xf - mu) * lax.rsqrt(var + LN_EPS) * gamma.astype(jnp.float32) + beta.astype(jnp.float32)
    return y.astype(x.dtype)

def dilated_window_attention(q, k, v, window, dilation):
    B, S, H, hd = q.shape
    steps = window // dilation
    span = steps * dilation
    Sp = -(-S // span) * span
    L = Sp // dilation
    nb = L // steps

    def to_blocks(t):
        t = jnp.pad(t, ((0, 0), (0, Sp - S), (0, 0), (0, 0)))
        t = t.reshape(B, L, dilation, H, hd).transpose(0, 2, 1, 3, 4)
        return t.reshape(B, dilation, nb, steps, H, hd)

    def with_prev(t):
        prev = jnp.pad(t[:, :, :-1], ((0, 0), (0, 0), (1, 0), (0, 0), (0, 0), (0, 0)))
        return jnp.concatenate([prev, t], axis=3)

    qb = to_blocks(q)
    kb = with_prev(to_blocks(k))
    vb = with_prev(to_blocks(v))
    scores = jnp.einsum('brnqhd,brnkhd->brnhqk', qb, kb,
                        preferred_element_type=jnp.float32) * (hd ** -0.5)
    qi = np.arange(steps)[:, None]
    kj = np.arange(2 * steps)[None, :]
    dist = steps + qi - kj
    blk = np.arange(nb)[:, None, None]
    mask = (dist >= 0) & (dist <= steps) & ((blk > 0) | (kj >= steps))[...]
    scores = jnp.where(jnp.asarray(mask)[None, None, :, None], scores, NEG_INF)
    m = jnp.max(scores, axis=-1, keepdims=True)
    e = jnp.exp(scores - m)
    den = jnp.sum(e, axis=-1)
    o = jnp.einsum('brnhqk,brnkhd->brnqhd', e.astype(v.dtype), vb,
                   preferred_element_type=jnp.float32)
    o = o / jnp.transpose(den, (0, 1, 2, 4, 3))[..., None]
    lse = m[..., 0] + jnp.log(den)
    o = o.reshape(B, dilation, L, H, hd).transpose(0, 2, 1, 3, 4).reshape(B, Sp, H, hd)[:, :S]
    lse = jnp.transpose(lse, (0, 1, 2, 4, 3)).reshape(B, dilation, L, H)
    lse = lse.transpose(0, 2, 1, 3).reshape(B, Sp, H)[:, :S]
    return o, lse

def causal_pool_mixer(u, w_pool, pool_scale):
    B, S, _ = u.shape
    uf = u.astype(jnp.float32)
    c = jnp.concatenate([jnp.zeros((B, 1, POOL_WIDTH), jnp.float32), jnp.cumsum(uf, axis=1)], axis=1)
    hi = np.arange(1, S + 1)
    outs = []
    for g, w in enumerate(POOL_WINDOWS):
        lo = np.maximum(hi - w, 0)
        cnt = np.minimum(hi, w).astype(np.float32)
        sl = slice(g * POOL_GROUP, (g + 1) * POOL_GROUP)
        window_sum = jnp.take(c[..., sl], hi, axis=1) - jnp.take(c[..., sl], lo, axis=1)
        outs.append(window_sum / jnp.asarray(cnt)[None, :, None] - uf[..., sl])
    p = jnp.stack(outs, axis=2).astype(u.dtype)
    y = jnp.einsum('bsgc,gcd->bsgd', p, w_pool).reshape(B, S, POOL_WIDTH)
    return y * pool_scale

def hybrid_layer(x, w_in, b_gate, w_pool, pool_scale, w_proj_attn, w_proj_pool, w_out, ln_gamma, ln_beta):
    B, S, _ = x.shape
    h = jnp.einsum('bsd,de->bse', x, w_in)
    idx = list(np.cumsum(SPLIT_SIZES)[:-1])
    q, k, v, z_attn, u_pool, z_pool, g_pre = jnp.split(h, idx, axis=-1)
    q = q.reshape(B, S, N_GROUPS, N_HEAD_SLOTS, HEAD_DIM)
    k = k.reshape(B, S, N_GROUPS, N_HEAD_SLOTS, HEAD_DIM)
    v = v.reshape(B, S, N_GROUPS, N_HEAD_SLOTS, HEAD_DIM)
    outs, lses = [], []
    for g, (window, dilation) in enumerate(DILATED_GROUPS):
        o_g, lse_g = dilated_window_attention(q[:, :, g], k[:, :, g], v[:, :, g], window, dilation)
        outs.append(o_g)
        lses.append(lse_g)
    wts = jax.nn.softmax(jnp.stack(lses, axis=0), axis=0)
    o = jnp.sum(wts[..., None] * jnp.stack(outs, axis=0), axis=0).reshape(B, S, ATTN_WIDTH)
    y_attn = o.astype(x.dtype) * jax.nn.silu(z_attn)
    y_pool = causal_pool_mixer(u_pool, w_pool, pool_scale) * jax.nn.silu(z_pool)
    gates = jax.nn.sigmoid((g_pre + b_gate).astype(jnp.float32)).astype(x.dtype)
    g_attn, g_pool = jnp.split(gates, 2, axis=-1)
    merged = g_attn * jnp.einsum('bsc,cd->bsd', y_attn, w_proj_attn) \
        + g_pool * jnp.einsum('bsc,cd->bsd', y_pool, w_proj_pool)
    out = jnp.einsum('bsd,de->bse', merged, w_out)
    return layer_norm(DEEPNORM_ALPHA * x + out, ln_gamma, ln_beta)

def setup_inputs(seed: int = 0) -> dict:
    key = jax.random.key(seed)
    ks = jax.random.split(key, 11)
    f32 = jnp.float32
    x = jax.random.normal(ks[0], (BATCH, SEQ, D_MODEL), f32)
    w_in = jax.random.normal(ks[1], (DEPTH, D_MODEL, IN_WIDTH), f32) * D_MODEL ** -0.5
    b_gate = jax.random.normal(ks[2], (DEPTH, N_BRANCHES * D_MODEL), f32) * 0.02
    w_pool = jax.random.normal(ks[3], (DEPTH, N_POOL_GROUPS, POOL_GROUP, POOL_GROUP), f32) * POOL_GROUP ** -0.5
    pool_scale = 1.0 + 0.02 * jax.random.normal(ks[4], (DEPTH, POOL_WIDTH), f32)
    w_proj_attn = jax.random.normal(ks[5], (DEPTH, ATTN_WIDTH, D_MODEL), f32) * ATTN_WIDTH ** -0.5 * DEEPNORM_BETA
    w_proj_pool = jax.random.normal(ks[6], (DEPTH, POOL_WIDTH, D_MODEL), f32) * POOL_WIDTH ** -0.5 * DEEPNORM_BETA
    w_out = jax.random.normal(ks[7], (DEPTH, D_MODEL, D_MODEL), f32) * D_MODEL ** -0.5 * DEEPNORM_BETA
    ln_gamma = 1.0 + 0.02 * jax.random.normal(ks[8], (DEPTH, D_MODEL), f32)
    ln_beta = 0.02 * jax.random.normal(ks[9], (DEPTH, D_MODEL), f32)
    return {"x": x, "w_in": w_in, "b_gate": b_gate, "w_pool": w_pool, "pool_scale": pool_scale,
            "w_proj_attn": w_proj_attn, "w_proj_pool": w_proj_pool, "w_out": w_out,
            "ln_gamma": ln_gamma, "ln_beta": ln_beta}

def reference(x, w_in, b_gate, w_pool, pool_scale, w_proj_attn, w_proj_pool, w_out, ln_gamma, ln_beta):
    for layer in range(DEPTH):
        x = hybrid_layer(x, w_in[layer], b_gate[layer], w_pool[layer], pool_scale[layer],
                         w_proj_attn[layer], w_proj_pool[layer], w_out[layer],
                         ln_gamma[layer], ln_beta[layer])
    return x


_drawn_inputs = setup_inputs


def setup_inputs(seed=0):
    import zlib

    import numpy as np

    out = dict(_drawn_inputs(seed))
    spreads = {}
    factors = {'b_gate': 8.0,
     'pool_scale': 8.0,
     'w_proj_attn': 3.109,
     'ln_gamma': 2.862,
     'ln_beta': 2.783}
    for name, (base, spread) in spreads.items():
        noise = np.random.default_rng([zlib.crc32(name.encode()), seed]).standard_normal(out[name].shape)
        drawn = base * np.exp(spread * noise) if base else spread * noise
        out[name] = __import__('jax').numpy.asarray(drawn.astype(out[name].dtype))
    for name, factor in factors.items():
        out[name] = (out[name] * factor).astype(out[name].dtype)
    return out
```

```python
from contextlib import ExitStack

import numpy as np

import concourse.bass as bass
from concourse import mybir

F32 = mybir.dt.float32
F32R = mybir.dt.float32r
ALU = mybir.AluOpType
ACT = mybir.ActivationFunctionType

P = 128
SEQ = 256
D_MODEL = 2048
HEADS = 8
HEAD_DIM = 128
DILATED = ((128, 1), (512, 4), (2048, 16))
GROUPS = len(DILATED)
POOL_WINDOWS = (2, 4, 8, 16)
POOL_GROUP = 256
ATTN_WIDTH = HEADS * HEAD_DIM
POOL_WIDTH = D_MODEL // 2
POOL_TILES = POOL_WIDTH // P
POOL_STEPS = 4
LN_EPS = 1e-5
ALPHA = 2.0 ** 0.25
SCALE = HEAD_DIM ** -0.5
NEG_INF = -1e30

TT = SEQ // P
KT = D_MODEL // P
OT = D_MODEL // P
HALF = KT // 2
CHUNK = KT * P
RING = 3
AHEAD = 2

A_STEPS, A_CHUNKS = HEADS, 12
B_STEPS, B_CHUNKS = 4, 12
POOL_MAP = A_STEPS * A_CHUNKS
B_FIRST = POOL_MAP + 1
C_FIRST = B_FIRST + B_STEPS * B_CHUNKS
CHUNKS = C_FIRST + OT
C_LOOP = 4
FROM = 1

Z_ATTN, V_FIRST, U_POOL, Z_POOL = 6, 7, 10, 11
SCORES_AFTER, PT_AFTER = 6, 8
A_EVACS = 8
B_EVACS = 8
S0 = GROUPS * P
S1 = GROUPS * SEQ
PTW = SEQ + P
PAD = 16


def layer_kernel(nc, xt_d, x_d, stream_d, bias_d, scale_d, gamma_d, beta_d, ident_d, mask_d,
                 coef_d, inv_d, out_d):
    with ExitStack() as ctx:
        def sem(name):
            return ctx.enter_context(nc.semaphore(name))

        def psum(name, shape):
            return ctx.enter_context(nc.psum_tensor(name, shape, F32))

        arena = ctx.enter_context(nc.sbuf_tensor("arena", [P, 206 * 256], F32))
        del arena
        base = nc.sbuf_base - 206 * 1024
        base = (base + 31) // 32 * 32

        def place(at, items):
            made = []
            for name, shape, dt in items:
                made.append(nc.alloc_sbuf_tensor_at(name, [P] + shape, dt, offset=at))
                at += 4 * int(np.prod(shape))
            return at, made

        at, (xt_hi, xt_lo, w_raw, w_hi, w_lo, ident, coef, gate_bias, half_bias, pool_scale,
             nmax, smax, den, rden, stats, mv, rstd, shift) = place(base, [
                 ("xt_hi", [KT, SEQ], F32R), ("xt_lo", [KT, SEQ], F32R),
                 ("w_raw", [RING, CHUNK], F32), ("w_hi", [RING, CHUNK], F32R),
                 ("w_lo", [RING, CHUNK], F32R), ("ident", [P], F32),
                 ("coef", [POOL_TILES * POOL_STEPS], F32), ("gate_bias", [2 * OT], F32),
                 ("half_bias", [2 * OT], F32), ("pool_scale", [POOL_TILES], F32),
                 ("nmax", [8], F32), ("smax", [8], F32), ("den", [8], F32), ("rden", [8], F32),
                 ("stats", [TT, OT, 6], F32), ("mv", [TT, 8], F32), ("rstd", [8], F32),
                 ("shift", [8], F32)])
        at_ya = at
        at, (ya_hi, ya_lo) = place(at_ya, [("ya_hi", [HEADS, SEQ], F32R),
                                           ("ya_lo", [HEADS, SEQ], F32R)])
        at_p = at
        at, (p_hi, p_lo) = place(at_p, [("p_hi", [POOL_TILES, SEQ], F32R),
                                        ("p_lo", [POOL_TILES, SEQ], F32R)])
        at, (szp, th_gate, tmp, sum_f) = place(at, [
            ("szp", [POOL_TILES, SEQ], F32), ("th_gate", [2, SEQ], F32),
            ("tmp", [2, SEQ], F32), ("sum_f", [SEQ], F32)])
        at_phase = at
        end_a, (q_hi, q_lo, k_hi, k_lo, vt_f, v_hi, v_lo, mask, s_sb, pt_hi, pt_lo, silu_za,
                u_pad, pool_a, pool_b, inv) = place(at_phase, [
                    ("q_hi", [GROUPS, SEQ], F32R), ("q_lo", [GROUPS, SEQ], F32R),
                    ("k_hi", [GROUPS, SEQ], F32R), ("k_lo", [GROUPS, SEQ], F32R),
                    ("vt_f", [GROUPS, SEQ], F32), ("v_hi", [GROUPS, SEQ], F32R),
                    ("v_lo", [GROUPS, SEQ], F32R), ("mask", [S0 + S1], F32),
                    ("s_sb", [S0 + S1], F32), ("pt_hi", [GROUPS, PTW], F32R),
                    ("pt_lo", [GROUPS, PTW], F32R), ("silu_za", [SEQ], F32),
                    ("u_pad", [PAD + SEQ], F32), ("pool_a", [PAD + SEQ], F32),
                    ("pool_b", [PAD + SEQ], F32), ("inv", [POOL_TILES, SEQ], F32)])
        _, (xt_raw,) = place(at_phase, [("xt_raw", [KT, SEQ], F32)])
        end_b, (yp_hi, yp_lo, merged_hi, merged_lo, yp_f) = place(at_phase, [
            ("yp_hi", [POOL_TILES, SEQ], F32R), ("yp_lo", [POOL_TILES, SEQ], F32R),
            ("merged_hi", [OT, SEQ], F32R), ("merged_lo", [OT, SEQ], F32R),
            ("yp_f", [2, 2 * SEQ], F32)])
        _, (res,) = place(at_p, [("res", [TT, D_MODEL], F32)])
        _, (gamma, beta) = place(at_ya, [("gamma", [D_MODEL], F32), ("beta", [D_MODEL], F32)])
        _, (ot_f,) = place(at_phase, [("ot_f", [RING, SEQ], F32)])
        assert max(end_a, end_b) <= nc.sbuf_usable_end, (end_a, end_b, nc.sbuf_usable_end)

        proj_ps = psum("proj_ps", [P, 2, 512])
        attn_ps = psum("attn_ps", [P, 4 * 512])
        turn_ps = psum("turn_ps", [P, 512])
        mixed_ps = psum("mixed_ps", [P, 512])

        x_landed = [sem(f"x_landed{q}") for q in range(4)]
        consts_landed = sem("consts_landed")
        tail_landed = sem("tail_landed")
        raw_landed = [sem(f"raw_landed{s}") for s in range(RING)]
        x_hi_done = sem("x_hi_done")
        x_lo_done = sem("x_lo_done")
        hi_split = sem("hi_split")
        lo_split = sem("lo_split")
        chunk_done = sem("chunk_done")
        act_evac = sem("act_evac")
        proj_free = sem("proj_free")
        bias_ready = sem("bias_ready")
        pads_zero = sem("pads_zero")
        scores_ready = sem("scores_ready")
        max_ready = sem("max_ready")
        exp_done = sem("exp_done")
        probs_ready = sem("probs_ready")
        vt_ready = sem("vt_ready")
        v_hi_done = sem("v_hi_done")
        v_split = sem("v_split")
        pt_ready = sem("pt_ready")
        pt_hi_done = sem("pt_hi_done")
        pt_split = sem("pt_split")
        mixed_ready = sem("mixed_ready")
        mixed_free = sem("mixed_free")
        y_split = sem("y_split")
        pool_split = sem("pool_split")
        pool_ready = sem("pool_ready")
        yp_f_ready = sem("yp_f_ready")
        yp_hi_done = sem("yp_hi_done")
        yp_split = sem("yp_split")
        merged_split = sem("merged_split")
        turned = sem("turned")
        turn_free = sem("turn_free")
        vec = sem("vec")
        var_ready = sem("var_ready")
        std_ready = sem("std_ready")
        shift_ready = sem("shift_ready")
        norm_done = sem("norm_done")
        out_ready = sem("out_ready")
        out_landed = sem("out_landed")

        N_CONSTS = 6
        CONSTS = 16 * N_CONSTS

        block = ctx.enter_context(nc.Block())

        def landed(eng, n, j, i, per):
            eng.wait_ge(raw_landed[(n + j) % RING], 16 * ((n + j) // RING + 1) + i * (16 * per // RING))

        @block.sync
        def _(sp):
            def load(slot, chunk):
                sp.dma_start(w_raw[:, slot, :], stream_d[chunk, :, :]).then_inc(raw_landed[slot], 16)

            def load_x(q):
                sp.dma_start(xt_raw[:, 4 * q:4 * q + 4, :], xt_d[q, :, :, :]).then_inc(x_landed[q], 16)

            load_x(0)
            load(0, 0)
            for q in range(1, 4):
                load_x(q)
            load(1, 1)
            load(2, 2)
            whole = (CHUNKS - RING) // RING
            with sp.Fori(0, whole) as i:
                for j in range(RING):
                    sp.wait_ge(lo_split, i * (2 * RING) + 2 * (j + 1))
                    sp.dma_start(w_raw[:, j, :],
                                 stream_d[bass.ds(i * RING + (RING + j), 1), :, :]
                                 .rearrange("a p n -> (a p) n")).then_inc(raw_landed[j], 16)
            for n in range(RING * (whole + 1), CHUNKS):
                sp.wait_ge(lo_split, 2 * (n - RING + 1))
                load(n % RING, n)

        @block.tensor
        def _(pe):
            mm, turn = nc.tensor.matmul, nc.tensor.transpose

            def product(out, a_hi, a_lo, b_hi, b_lo, first=True, last=True):
                mm(out, a_hi, b_hi, start=first, stop=False)
                mm(out, a_hi, b_lo, start=False, stop=False)
                return mm(out, a_lo, b_hi, start=False, stop=last)

            def chunk(n, j, i, per, moving, between=None):
                slot = (n + j) % RING
                for half in range(2):
                    pe.wait_ge(lo_split, 2 * (n + j) + half + 1 + i * (2 * per))
                    for k in range(half * HALF, (half + 1) * HALF):
                        if between:
                            between(k)
                        out, hi, lo, first, last = moving(k)
                        cols = slice(k * P, (k + 1) * P)
                        done = product(out, w_hi[:, slot, cols], w_lo[:, slot, cols], hi, lo, first, last)
                done.then_inc(chunk_done, 1)

            def next_bank(n, j, i, per):
                pe.wait_ge(proj_free, FROM + n + j + i * per)

            def from_x(bank):
                return lambda k: (proj_ps[:, bank, 0:SEQ], xt_hi[:, k, :], xt_lo[:, k, :],
                                  k == 0, k == KT - 1)

            def x_arrives(k):
                if k % 4 == 0:
                    pe.wait_ge(x_lo_done, k // 4 + 1)

            def scores(i):
                pe.wait_ge(pt_split, FROM + i * GROUPS)
                for t in range(TT):
                    for g in range(GROUPS):
                        at = g * P if t == 0 else 512 + g * SEQ
                        keys = (t + 1) * P
                        q = slice(t * P, (t + 1) * P)
                        done = product(attn_ps[:, at:at + keys], q_hi[:, g, q], q_lo[:, g, q],
                                       k_hi[:, g, 0:keys], k_lo[:, g, 0:keys])
                done.then_inc(scores_ready, 1)

            def turn_probs(i):
                pe.wait_ge(consts_landed, CONSTS)
                pe.wait_ge(probs_ready, i * 2 + 2)
                for g in range(GROUPS):
                    at = g * 512
                    turn(attn_ps[:, at:at + P], s_sb[:, g * P:(g + 1) * P], ident[:, :])
                    for kt in range(2):
                        src = S0 + g * SEQ + kt * P
                        done = turn(attn_ps[:, at + P + kt * P:at + 2 * P + kt * P],
                                    s_sb[:, src:src + P], ident[:, :])
                    done.then_inc(pt_ready, 1)

            def turn_v(i, g):
                pe.wait_ge(v_split, FROM + i * GROUPS + g)
                for t in range(TT):
                    done = turn(turn_ps[:, t * P:(t + 1) * P], vt_f[:, g, t * P:(t + 1) * P], ident[:, :])
                done.then_inc(vt_ready, 1)

            def mix(i):
                pe.wait_ge(pt_split, FROM + i * GROUPS + GROUPS)
                pe.wait_ge(v_split, FROM + i * GROUPS + GROUPS)
                pe.wait_ge(mixed_free, FROM + i)
                for g in range(GROUPS):
                    for kt in range(TT):
                        out = mixed_ps[:, 0:SEQ] if kt == 0 else mixed_ps[:, P:SEQ]
                        pcols = slice(0, SEQ) if kt == 0 else slice(SEQ, PTW)
                        v = slice(kt * P, (kt + 1) * P)
                        done = product(out, v_hi[:, g, v], v_lo[:, g, v], pt_hi[:, g, pcols],
                                       pt_lo[:, g, pcols], first=(g == 0 and kt == 0),
                                       last=(g == GROUPS - 1 and kt == TT - 1))
                done.then_inc(mixed_ready, 1)

            pe.sem_inc(chunk_done, FROM)
            with pe.Fori(0, A_STEPS) as i:
                for j in range(A_CHUNKS):
                    chunk(0, j, i, A_CHUNKS, from_x(j % 2), x_arrives if j == 0 else None)
                    next_bank(0, j, i, A_CHUNKS)
                    if j == SCORES_AFTER:
                        scores(i)
                    if j == PT_AFTER:
                        turn_probs(i)
                    if 0 <= j - V_FIRST - 1 < GROUPS:
                        turn_v(i, j - V_FIRST - 1)
                mix(i)

            pe.wait_ge(lo_split, 2 * POOL_MAP + 2)
            pe.wait_ge(pool_split, POOL_TILES)
            slot = POOL_MAP % RING
            for g in range(POOL_TILES // 2):
                for m in range(2):
                    for kk in range(2):
                        cols = slice((g * 2 + kk) * POOL_GROUP + m * P, (g * 2 + kk) * POOL_GROUP + (m + 1) * P)
                        last = product(attn_ps[:, g * 512 + m * SEQ:g * 512 + (m + 1) * SEQ],
                                       w_hi[:, slot, cols], w_lo[:, slot, cols],
                                       p_hi[:, 2 * g + kk, :], p_lo[:, 2 * g + kk, :],
                                       first=(kk == 0), last=(kk == 1))
                last.then_inc(pool_ready if g < POOL_TILES // 2 - 1 else chunk_done, 1)
            next_bank(POOL_MAP, 0, 0, 0)

            def from_y(bank):
                def moving(k):
                    out = proj_ps[:, bank, 0:SEQ] if k < HALF else proj_ps[:, bank, SEQ:2 * SEQ]
                    hi, lo = (ya_hi, ya_lo) if k < HALF else (yp_hi, yp_lo)
                    return out, hi[:, k % HALF, :], lo[:, k % HALF, :], k % HALF == 0, k % HALF == HALF - 1
                return moving

            with pe.Fori(0, B_STEPS) as i:
                for j in range(B_CHUNKS):
                    bank = (B_FIRST + j) % 2
                    if j % 3 < 2:
                        chunk(B_FIRST, j, i, B_CHUNKS, from_x(bank))
                    else:
                        pe.wait_ge(y_split, HEADS)
                        pe.wait_ge(yp_split, POOL_TILES // 2)
                        chunk(B_FIRST, j, i, B_CHUNKS, from_y(bank))
                    next_bank(B_FIRST, j, i, B_CHUNKS)

            def from_merged(bank):
                return lambda k: (proj_ps[:, bank, 0:SEQ], merged_hi[:, k, :], merged_lo[:, k, :],
                                  k == 0, k == KT - 1)

            def merged_arrives(k):
                if k in (0, KT - 1):
                    pe.wait_ge(merged_split, OT - 1 if k == 0 else OT)

            def turn_out(e, slot, i):
                pe.wait_ge(turn_free, FROM + e + i * RING)
                for t in range(TT):
                    done = turn(turn_ps[:, t * P:(t + 1) * P], ot_f[:, slot, t * P:(t + 1) * P], ident[:, :])
                done.then_inc(turned, 1)

            chunk(C_FIRST, 0, 0, 0, from_merged(C_FIRST % 2), merged_arrives)
            next_bank(C_FIRST, 0, 0, 0)

            def c_step(e, i, per, bank):
                chunk(C_FIRST, e, i, per, from_merged(bank))
                next_bank(C_FIRST, e, i, per)
                turn_out(e - 1, (e - 1) % RING, i)

            with pe.Fori(0, C_LOOP // 2) as i:
                for j in range(2 * RING):
                    chunk(C_FIRST + 1, j, i, 2 * RING, from_merged((C_FIRST + 1 + j) % 2))
                    next_bank(C_FIRST + 1, j, i, 2 * RING)
                    pe.wait_ge(turn_free, FROM + j + i * (2 * RING))
                    for t in range(TT):
                        done = turn(turn_ps[:, t * P:(t + 1) * P], ot_f[:, j % RING, t * P:(t + 1) * P],
                                    ident[:, :])
                    done.then_inc(turned, 1)
            for e in range(C_LOOP * RING + 1, OT):
                c_step(e, 0, 0, (C_FIRST + e) % 2)
            next_bank(C_FIRST, OT, 0, 0)
            turn_out(OT - 1, (OT - 1) % RING, 0)

        @block.scalar
        def _(act):
            activation = nc.scalar.activation


            def split_hi(n, j, i, per):
                slot = (n + j) % RING
                landed(act, n, j, i, per)
                if n or j >= RING or per:
                    act.wait_ge(chunk_done, FROM + n + j - AHEAD + i * per)
                for half in range(2):
                    cols = slice(half * HALF * P, (half + 1) * HALF * P)
                    activation(w_hi[:, slot, cols], w_raw[:, slot, cols], ACT.Copy).then_inc(hi_split, 1)

            def done_chunk(n, j, i, per):
                act.wait_ge(chunk_done, FROM + n + j + 1 + i * per)

            for q in range(4):
                act.wait_ge(x_landed[q], 16)
                activation(xt_hi[:, 4 * q:4 * q + 4, :], xt_raw[:, 4 * q:4 * q + 4, :],
                           ACT.Copy).then_inc(x_hi_done, 1)
                if q == 0:
                    split_hi(0, 0, 0, 0)
            for dst, src in ((ident[:, :], ident_d), (coef[:, :], coef_d), (gate_bias[:, :], bias_d),
                             (pool_scale[:, :], scale_d), (mask[:, :], mask_d), (inv[:, :, :], inv_d)):
                act.dma_start(dst, src).then_inc(consts_landed, 16)
            split_hi(0, 1, 0, 0)

            def exp_probs(i):
                act.wait_ge(max_ready, i + 1)
                for t, cols in ((0, slice(0, S0)), (1, slice(S0, S0 + S1))):
                    activation(s_sb[:, cols], s_sb[:, cols], ACT.Exp, bias=nmax[:, t:t + 1], scale=SCALE,
                               accum_out=den[:, t:t + 1]).then_inc(exp_done, 1)

            def v_hi_part(i, g):
                act.wait_ge(vt_ready, i * GROUPS + g + 1)
                activation(v_hi[:, g, :], turn_ps[:, 0:SEQ], ACT.Copy).then_inc(v_hi_done, 1)

            with act.Fori(0, A_STEPS) as i:
                for j in range(A_CHUNKS):
                    if j == V_FIRST:
                        exp_probs(i)
                    if j == V_FIRST + 2:
                        for g in range(GROUPS):
                            act.wait_ge(pt_ready, i * GROUPS + g + 1)
                            activation(pt_hi[:, g, :], attn_ps[:, g * 512:g * 512 + PTW],
                                       ACT.Copy).then_inc(pt_hi_done, 1)
                    if 0 <= j - V_FIRST - 2 < GROUPS:
                        v_hi_part(i, j - V_FIRST - 2)
                    split_hi(0, j + AHEAD, i, A_CHUNKS)
                    if j < Z_ATTN:
                        done_chunk(0, j, i, A_CHUNKS)
                        dst = (q_hi, k_hi)[j % 2]
                        activation(dst[:, j // 2, :], proj_ps[:, j % 2, 0:SEQ], ACT.Copy).then_inc(act_evac, 1)
                    if j in (Z_ATTN, Z_POOL):
                        done_chunk(0, j, i, A_CHUNKS)
                        act.wait_ge(proj_free, FROM + j - 1 + i * A_CHUNKS)
                        activation(th_gate[:, int(j == Z_POOL), :], proj_ps[:, j % 2, 0:SEQ], ACT.Tanh,
                                   scale=0.5).then_inc(act_evac, 1)

            split_hi(POOL_MAP, AHEAD, 0, 0)
            act.wait_ge(chunk_done, FROM + POOL_MAP + 1)
            act.dma_start(res[:, :, :], x_d).then_inc(tail_landed, 16)
            for g in range(POOL_TILES // 2):
                act.wait_ge(yp_f_ready, g + 1)
                activation(yp_hi[:, 2 * g:2 * g + 2, :], yp_f[:, g % 2, :], ACT.Copy).then_inc(yp_hi_done, 1)
            act.wait_ge(bias_ready, 1)
            with act.Fori(0, B_STEPS) as i:
                for j in range(B_CHUNKS):
                    split_hi(B_FIRST, j + AHEAD, i, B_CHUNKS)
                    if j % 3 < 2:
                        done_chunk(B_FIRST, j, i, B_CHUNKS)
                        act.wait_ge(proj_free, FROM + B_FIRST + j - 2 + i * B_CHUNKS)
                        activation(th_gate[:, j % 3, :], proj_ps[:, (B_FIRST + j) % 2, 0:SEQ], ACT.Tanh,
                                   bias=half_bias[:, bass.ds(i * 4 + ((j % 3) * OT + j // 3), 1)],
                                   scale=0.5).then_inc(act_evac, 1)
            act.wait_ge(chunk_done, FROM + C_FIRST)
            act.dma_start(gamma[:, :], gamma_d).then_inc(tail_landed, 16)
            act.dma_start(beta[:, :], beta_d).then_inc(tail_landed, 16)
            split_hi(C_FIRST, AHEAD, 0, 0)
            with act.Fori(0, C_LOOP) as i:
                for j in range(RING):
                    split_hi(C_FIRST + 1, j + AHEAD, i, RING)
            split_hi(C_FIRST + C_LOOP * RING + 1, AHEAD, 0, 0)
            for t in range(TT):
                act.wait_ge(var_ready, t + 1)
                activation(rstd[:, t:t + 1], mv[:, t, 2:3], ACT.Sqrt).then_inc(std_ready, 1)
            for t in range(TT):
                act.wait_ge(shift_ready, t + 1)
                for c in range(4):
                    cols = slice(c * 512, (c + 1) * 512)
                    activation(res[:, t, cols], res[:, t, cols], ACT.Identity, bias=shift[:, t:t + 1],
                               scale=rstd[:, 2 + t:3 + t]).then_inc(norm_done, 1)
            for t in range(TT):
                for c in range(2):
                    act.wait_ge(out_ready, (t * 2 + c + 1) * 2)
                    cols = slice(c * 1024, (c + 1) * 1024)
                    act.dma_start(out_d[t, :, cols], res[:, t, cols]).then_inc(out_landed, 16)
            act.wait_ge(out_landed, 16 * 2 * TT)

        @block.vector
        def _(dve):
            tt, ts = nc.vector.tensor_tensor, nc.vector.tensor_scalar
            stt, copy = nc.vector.scalar_tensor_tensor, nc.vector.tensor_copy

            class Chain:
                count, per, i = 0, 0, 0

                def ready(self):
                    dve.wait_ge(vec, self.count + (self.i * self.per if self.per else 0))

                def add(self, ins):
                    ins.then_inc(vec, 1)
                    self.count += 1

                def link(self, ins):
                    self.add(ins)
                    self.ready()

            chain = Chain()
            for freed in (proj_free, pt_split, v_split, mixed_free, turn_free):
                dve.sem_inc(freed, FROM)

            def split_lo(n, j, i, per):
                slot = (n + j) % RING
                for half in range(2):
                    dve.wait_ge(hi_split, 2 * (n + j) + half + 1 + i * (2 * per))
                    cols = slice(half * HALF * P, (half + 1) * HALF * P)
                    tt(w_lo[:, slot, cols], w_raw[:, slot, cols], w_hi[:, slot, cols].bitcast(F32),
                       ALU.subtract).then_inc(lo_split, 1)

            def done_chunk(n, j, i, per):
                dve.wait_ge(chunk_done, FROM + n + j + 1 + i * per)

            for q in range(4):
                dve.wait_ge(x_hi_done, q + 1)
                tt(xt_lo[:, 4 * q:4 * q + 4, :], xt_raw[:, 4 * q:4 * q + 4, :],
                   xt_hi[:, 4 * q:4 * q + 4, :].bitcast(F32), ALU.subtract).then_inc(x_lo_done, 1)
                if q == 0:
                    split_lo(0, 0, 0, 0)
            for pad in (u_pad, pool_a, pool_b):
                chain.link(nc.vector.memset(pad[:, 0:PAD], 0.0))
            split_lo(0, 1, 0, 0)

            def silu(j, i, last):
                dve.wait_ge(act_evac, i * A_EVACS + (7 if j == Z_ATTN else 8))
                chain.link(ts(tmp[:, 0, :], th_gate[:, int(j == Z_POOL), :], 0.5, 0.5, ALU.mult, ALU.add))
                last().then_inc(proj_free, 1)

            def masked_max(i):
                dve.wait_ge(scores_ready, i + 1)
                dve.wait_ge(consts_landed, CONSTS)
                chain.add(nc.vector.memset(smax[:, 4:6], 0.0))
                for t, at, cols in ((0, 0, slice(0, S0)), (1, 512, slice(S0, S0 + S1))):
                    chain.add(nc.vector.tensor_tensor_reduce(
                        s_sb[:, cols], attn_ps[:, at:at + cols.stop - cols.start], mask[:, cols], 1.0,
                        -3.0e38, ALU.add, ALU.max, smax[:, t:t + 1]))
                chain.ready()
                ts(nmax[:, 0:2], smax[:, 0:2], -SCALE, None, ALU.mult).then_inc(max_ready, 1)

            def normalise(i):
                dve.wait_ge(exp_done, i * 2 + 2)
                chain.link(nc.vector.reciprocal(rden[:, 0:2], den[:, 0:2]))
                for t, cols in ((0, slice(0, S0)), (1, slice(S0, S0 + S1))):
                    ts(s_sb[:, cols], s_sb[:, cols], rden[:, t:t + 1], None, ALU.mult).then_inc(probs_ready, 1)

            def pool(h):
                src = u_pad
                for k, dst in enumerate((pool_a, pool_b, pool_a, pool_b)):
                    back = PAD - 2 ** k
                    chain.link(stt(out=dst[:, PAD:PAD + SEQ], in0=src[:, back:back + SEQ],
                                   scalar=coef[:, bass.ds(h * POOL_STEPS + k, 1)],
                                   in1=src[:, PAD:PAD + SEQ], op0=ALU.mult, op1=ALU.add))
                    src = dst
                chain.link(tt(pool_a[:, PAD:PAD + SEQ], src[:, PAD:PAD + SEQ],
                              inv[:, bass.ds(h, 1), :].rearrange("p a s -> p (a s)"), ALU.mult))
                chain.link(tt(tmp[:, 1, :], pool_a[:, PAD:PAD + SEQ], u_pad[:, PAD:PAD + SEQ], ALU.subtract))
                split(tmp[:, 1, :], p_hi, p_lo, h, pool_split)

            def split(src, hi, lo, tile, signal):
                def at(t):
                    return t[:, bass.ds(tile, 1), :].rearrange("p a s -> p (a s)")
                chain.link(copy(at(hi), src))
                tt(at(lo), src, at(hi).bitcast(F32), ALU.subtract).then_inc(signal, 1)

            per_a = 14
            start_a = chain.count
            with dve.Fori(0, A_STEPS) as i:
                chain.i, chain.per = i, per_a
                for j in range(A_CHUNKS):
                    bank = proj_ps[:, j % 2, 0:SEQ]
                    if j == V_FIRST:
                        normalise(i)
                    if j == V_FIRST + 2:
                        for g in range(GROUPS):
                            dve.wait_ge(pt_hi_done, i * GROUPS + g + 1)
                            tt(pt_lo[:, g, :], attn_ps[:, g * 512:g * 512 + PTW],
                               pt_hi[:, g, :].bitcast(F32), ALU.subtract).then_inc(pt_split, 1)
                    if 0 <= j - V_FIRST - 2 < GROUPS:
                        g = j - V_FIRST - 2
                        dve.wait_ge(v_hi_done, i * GROUPS + g + 1)
                        tt(v_lo[:, g, :], turn_ps[:, 0:SEQ], v_hi[:, g, :].bitcast(F32),
                           ALU.subtract).then_inc(v_split, 1)
                    split_lo(0, j + AHEAD, i, A_CHUNKS)
                    if j < Z_ATTN:
                        hi, lo = ((q_hi, q_lo), (k_hi, k_lo))[j % 2]
                        dve.wait_ge(act_evac, i * A_EVACS + j + 1)
                        tt(lo[:, j // 2, :], bank, hi[:, j // 2, :].bitcast(F32),
                           ALU.subtract).then_inc(proj_free, 1)
                    if j == Z_ATTN:
                        silu(j, i, lambda: tt(silu_za[:, :], bank, tmp[:, 0, :], ALU.mult))
                        masked_max(i)
                    if V_FIRST <= j < V_FIRST + GROUPS:
                        done_chunk(0, j, i, A_CHUNKS)
                        copy(vt_f[:, j - V_FIRST, :], bank).then_inc(proj_free, 1)
                    if j == U_POOL:
                        done_chunk(0, j, i, A_CHUNKS)
                        copy(u_pad[:, PAD:PAD + SEQ], bank).then_inc(proj_free, 1)
                    if j == Z_POOL:
                        silu(j, i, lambda: stt(
                            out=szp[:, bass.ds(i, 1), :].rearrange("p a s -> p (a s)"), in0=bank,
                            scalar=pool_scale[:, bass.ds(i, 1)], in1=tmp[:, 0, :],
                            op0=ALU.mult, op1=ALU.mult))
                dve.wait_ge(proj_free, FROM + U_POOL + 1 + i * A_CHUNKS)
                pool(i)
                dve.wait_ge(mixed_ready, i + 1)
                tt(sum_f[:, :], mixed_ps[:, 0:SEQ], silu_za[:, :], ALU.mult).then_inc(mixed_free, 1)
                dve.wait_ge(mixed_free, FROM + i + 1)
                split(sum_f[:, :], ya_hi, ya_lo, i, y_split)
            assert chain.count - start_a == per_a, chain.count - start_a
            chain.count, chain.per = start_a + per_a * A_STEPS, 0

            split_lo(POOL_MAP, AHEAD, 0, 0)
            ts(half_bias[:, :], gate_bias[:, :], 0.5, None, ALU.mult).then_inc(bias_ready, 1)
            for g in range(POOL_TILES // 2):
                if g < POOL_TILES // 2 - 1:
                    dve.wait_ge(pool_ready, g + 1)
                else:
                    dve.wait_ge(chunk_done, FROM + POOL_MAP + 1)
                if g >= 2:
                    dve.wait_ge(yp_split, g - 1)
                tt(yp_f[:, g % 2, :], attn_ps[:, g * 512:(g + 1) * 512],
                   szp[:, 2 * g:2 * g + 2, :].rearrange("p a s -> p (a s)"), ALU.mult).then_inc(yp_f_ready, 1)
                if g % 2 == 1:
                    for b in (g - 1, g):
                        dve.wait_ge(yp_hi_done, b + 1)
                        tt(yp_lo[:, 2 * b:2 * b + 2, :].rearrange("p a s -> p (a s)"), yp_f[:, b % 2, :],
                           yp_hi[:, 2 * b:2 * b + 2, :].rearrange("p a s -> p (a s)").bitcast(F32),
                           ALU.subtract).then_inc(yp_split, 1)
            nc.vector.memset(smax[:, 6:8], 0.0).then_inc(proj_free, 1)

            per_b = 4 * 3
            start_b = chain.count
            with dve.Fori(0, B_STEPS) as i:
                chain.i, chain.per = i, per_b
                for j in range(B_CHUNKS):
                    split_lo(B_FIRST, j + AHEAD, i, B_CHUNKS)
                    bank = (B_FIRST + j) % 2
                    gate = j % 3
                    if gate < 2:
                        dve.wait_ge(act_evac, A_STEPS * A_EVACS + i * B_EVACS + (j // 3) * 2 + gate + 1)
                        ts(tmp[:, gate, :], th_gate[:, gate, :], 0.5, 0.5, ALU.mult,
                           ALU.add).then_inc(proj_free, 1)
                    else:
                        done_chunk(B_FIRST, j, i, B_CHUNKS)
                        dve.wait_ge(proj_free, FROM + B_FIRST + j + i * B_CHUNKS)
                        chain.add(tt(szp[:, 0, :], proj_ps[:, bank, 0:SEQ], tmp[:, 0, :], ALU.mult))
                        tt(szp[:, 1, :], proj_ps[:, bank, SEQ:2 * SEQ], tmp[:, 1, :],
                           ALU.mult).then_inc(proj_free, 1)
                        dve.wait_ge(proj_free, FROM + B_FIRST + j + 1 + i * B_CHUNKS)
                        chain.ready()
                        chain.link(tt(sum_f[:, :], szp[:, 0, :], szp[:, 1, :], ALU.add))
                        tile = i * 4 + j // 3
                        split(sum_f[:, :], merged_hi, merged_lo, tile, merged_split)
            assert chain.count - start_b == per_b, chain.count - start_b
            chain.count, chain.per = start_b + per_b * B_STEPS, 0

            def copy_out(e, slot, i, per):
                done_chunk(C_FIRST, e, i, per)
                copy(ot_f[:, slot, :], proj_ps[:, (C_FIRST + e) % 2, 0:SEQ]).then_inc(proj_free, 1)

            def residual(e, count, i, per, tile):
                dve.wait_ge(turned, count + i * per)
                at = res[:, :, bass.ds(tile * P, P)]
                stt(out=at, in0=at, scalar=ALPHA, in1=turn_ps[:, 0:SEQ].rearrange("p (t c) -> p t c", t=TT),
                    op0=ALU.mult, op1=ALU.add).then_inc(turn_free, 1)
                dve.wait_ge(turn_free, FROM + count + i * per)
                for t in range(TT):
                    out = stats[:, t, bass.ds(tile, 1), :].rearrange("p a s -> p (a s)")
                    chain.add(nc.vector.bn_stats(
                        out, res[:, t, bass.ds(tile * P, P)]))

            split_lo(C_FIRST, AHEAD, 0, 0)
            copy_out(0, 0, 0, 0)
            dve.wait_ge(tail_landed, 16 * 3)
            per_c = 2 * RING * TT
            start_c = chain.count
            with dve.Fori(0, C_LOOP // 2) as i:
                chain.i, chain.per = i, per_c
                for j in range(2 * RING):
                    split_lo(C_FIRST + 1, j + AHEAD, i, 2 * RING)
                    residual(j, j + 1, i, 2 * RING, i * (2 * RING) + j)
                    copy_out(j + 1, (j + 1) % RING, i, 2 * RING)
            assert chain.count - start_c == per_c
            chain.count, chain.per = start_c + per_c * (C_LOOP // 2), 0
            for e in range(C_LOOP * RING + 1, OT):
                if C_FIRST + e + AHEAD < CHUNKS:
                    split_lo(C_FIRST, e + AHEAD, 0, 0)
                residual(e - 1, e, 0, 0, e - 1)
                copy_out(e, e % RING, 0, 0)
            residual(OT - 1, OT, 0, 0, OT - 1)
            chain.ready()

            for t in range(TT):
                chain.link(nc.vector.bn_aggr(mv[:, t, 0:2], stats[:, t, :, :].rearrange("p a s -> p (a s)")))
                ts(mv[:, t, 2:3], mv[:, t, 1:2], LN_EPS, None, ALU.add).then_inc(var_ready, 1)
            for t in range(TT):
                dve.wait_ge(std_ready, t + 1)
                chain.link(nc.vector.reciprocal(rstd[:, 2 + t:3 + t], rstd[:, t:t + 1]))
                stt(out=shift[:, t:t + 1], in0=mv[:, t, 0:1], scalar=-1.0, in1=rstd[:, 2 + t:3 + t],
                    op0=ALU.mult, op1=ALU.mult).then_inc(shift_ready, 1)
            for t in range(TT):
                for c in range(4):
                    cols = slice(c * 512, (c + 1) * 512)
                    dve.wait_ge(norm_done, t * 4 + c + 1)
                    chain.link(tt(res[:, t, cols], res[:, t, cols], gamma[:, cols], ALU.mult))
                    tt(res[:, t, cols], res[:, t, cols], beta[:, cols], ALU.add).then_inc(out_ready, 1)


def _mask():
    t, s = np.arange(SEQ)[:, None], np.arange(SEQ)[None, :]
    tiles = []
    for tile in range(TT):
        for window, dilation in DILATED:
            sees = (s <= t) & (t - s <= window) & ((t - s) % dilation == 0)
            m = np.where(sees, 0.0, NEG_INF).astype(np.float32)
            tiles.append(m[tile * P:(tile + 1) * P, :(tile + 1) * P])
    return np.ascontiguousarray(np.concatenate(tiles, axis=1))


def _pool_tables():
    coef = np.zeros((POOL_TILES, POOL_STEPS), np.float32)
    inv = np.zeros((POOL_TILES, SEQ), np.float32)
    for tile in range(POOL_TILES):
        w = POOL_WINDOWS[tile * P // POOL_GROUP]
        coef[tile, :int(np.log2(w))] = 1.0
        inv[tile] = 1.0 / np.minimum(np.arange(1, SEQ + 1), w).astype(np.float32)
    return (np.ascontiguousarray(np.broadcast_to(coef.reshape(1, -1), (P, POOL_TILES * POOL_STEPS))),
            np.ascontiguousarray(np.broadcast_to(inv.reshape(1, POOL_TILES, SEQ), (P, POOL_TILES, SEQ))))


def _tiles(w):
    k, n = w.shape
    return w.reshape(k // P, P, n // P, P).transpose(2, 1, 0, 3)


def _stream(w_in, w_pool, w_proj_attn, w_proj_pool, w_out):
    cols = _tiles(w_in)
    qkv = GROUPS * HEADS
    z_attn, u_pool, z_pool = 3 * qkv, 3 * qkv + HEADS, 3 * qkv + HEADS + POOL_TILES
    gates = z_pool + POOL_TILES
    stream = np.empty((CHUNKS, P, CHUNK), np.float32)
    n = 0
    for h in range(HEADS):
        order = [part * qkv + g * HEADS + h for g in range(GROUPS) for part in range(2)]
        order += [z_attn + h] + [2 * qkv + g * HEADS + h for g in range(GROUPS)] + [u_pool + h, z_pool + h]
        for tile in order:
            stream[n] = cols[tile].reshape(P, CHUNK)
            n += 1
    stream[n] = w_pool.reshape(4, 2, P, POOL_GROUP).transpose(2, 0, 1, 3).reshape(P, CHUNK)
    n += 1
    attn, pool, last = _tiles(w_proj_attn), _tiles(w_proj_pool), _tiles(w_out)
    for d in range(OT):
        stream[n] = cols[gates + d].reshape(P, CHUNK)
        stream[n + 1] = cols[gates + OT + d].reshape(P, CHUNK)
        stream[n + 2] = np.concatenate([attn[d], pool[d]], axis=1).reshape(P, CHUNK)
        n += 3
    for e in range(OT):
        stream[n] = last[e].reshape(P, CHUNK)
        n += 1
    return stream


def kernel(x, w_in, b_gate, w_pool, pool_scale, w_proj_attn, w_proj_pool, w_out, ln_gamma, ln_beta):
    import concourse.bacc as bacc
    from concourse.bass_utils import run_bass_kernel_spmd

    x = np.asarray(x)[0]
    w_in, b_gate, w_pool, pool_scale, w_proj_attn, w_proj_pool, w_out, ln_gamma, ln_beta = (
        np.asarray(a)[0] for a in (w_in, b_gate, w_pool, pool_scale, w_proj_attn, w_proj_pool, w_out,
                                   ln_gamma, ln_beta))
    coef, inv = _pool_tables()
    arrays = {
        "xt": x.T.reshape(4, 4, P, SEQ).transpose(0, 2, 1, 3),
        "x_rows": x.reshape(TT, P, D_MODEL).transpose(1, 0, 2),
        "weights": _stream(w_in, w_pool, w_proj_attn, w_proj_pool, w_out),
        "gate_bias": b_gate.reshape(2 * OT, P).T,
        "pool_scale": pool_scale.reshape(POOL_TILES, P).T,
        "gamma_row": ln_gamma.reshape(1, D_MODEL).repeat(P, axis=0),
        "beta_row": ln_beta.reshape(1, D_MODEL).repeat(P, axis=0),
        "identity": np.eye(P, dtype=np.float32),
        "mask": _mask(),
        "pool_coef": coef,
        "pool_inv": inv,
    }
    arrays = {f"in_{k}": np.ascontiguousarray(v) for k, v in arrays.items()}
    nc = bacc.Bacc("TRN2", target_bir_lowering=False, num_devices=1)
    args = [nc.dram_tensor(k, v.shape, mybir.dt.from_np(v.dtype), kind="ExternalInput").ap()
            for k, v in arrays.items()]
    args.append(nc.dram_tensor("out_rows", (TT, P, D_MODEL), F32, kind="ExternalOutput").ap())
    layer_kernel(nc, *args)
    r = run_bass_kernel_spmd(nc, [arrays], core_ids=[0])
    return r.results[0]["out_rows"].reshape(1, SEQ, D_MODEL)
```

```python
from contextlib import ExitStack

import numpy as np

import concourse.bass as bass
from concourse import mybir

F32 = mybir.dt.float32
F32R = mybir.dt.float32r
ALU = mybir.AluOpType
ACT = mybir.ActivationFunctionType

P = 128
SEQ = 256
D_MODEL = 2048
HEADS = 8
HEAD_DIM = 128
DILATED = ((128, 1), (512, 4), (2048, 16))
GROUPS = len(DILATED)
POOL_WINDOWS = (2, 4, 8, 16)
POOL_GROUP = 256
ATTN_WIDTH = HEADS * HEAD_DIM
POOL_WIDTH = D_MODEL // 2
POOL_TILES = POOL_WIDTH // P
POOL_STEPS = 4
POOL_COEFS = POOL_STEPS + 1
LN_EPS = 1e-5
ALPHA = 2.0 ** 0.25
SCALE = HEAD_DIM ** -0.5
NEG_INF = -1e30

TT = SEQ // P
KT = D_MODEL // P
OT = D_MODEL // P
HALF = KT // 2
CHUNK = KT * P
RING = 3
AHEAD = 2

A_STEPS, A_CHUNKS = HEADS, 12
B_STEPS, B_CHUNKS = 4, 12
A_BANKED = A_CHUNKS - GROUPS
POOL_MAP = A_STEPS * A_CHUNKS
B_FIRST = POOL_MAP + 1
C_FIRST = B_FIRST + B_STEPS * B_CHUNKS
CHUNKS = C_FIRST + OT
BLOCK = 512
BLOCKS = D_MODEL // BLOCK
BLOCK_CHUNKS = OT // BLOCKS
BLOCK_KT = KT // BLOCK_CHUNKS
FROM = 1

Z_ATTN, V_FIRST, U_POOL, Z_POOL = 6, 7, 10, 11
SCORES_AFTER, PT_AFTER = 6, 8
S0 = GROUPS * P
S1 = GROUPS * SEQ
PTW = SEQ + P
PAD = 16


def banked(n, j):
    if n == 0:
        return j - min(max(j - V_FIRST, 0), GROUPS)
    return A_STEPS * A_BANKED + n - B_FIRST + j


def banked_per(n):
    return A_BANKED if n == 0 else B_CHUNKS


def layer_kernel(nc, xt_d, x_d, stream_d, bias_d, scale_d, gamma_d, gamma_beta_d, ident_d, mask_d,
                 coef_d, inv_d, out_d):
    with ExitStack() as ctx:
        def sem(name):
            return ctx.enter_context(nc.semaphore(name))

        def psum(name, shape):
            return ctx.enter_context(nc.psum_tensor(name, shape, F32))

        arena = ctx.enter_context(nc.sbuf_tensor("arena", [P, 206 * 256], F32))
        del arena
        base = nc.sbuf_base - 206 * 1024
        base = (base + 31) // 32 * 32

        def place(at, items):
            made = []
            for name, shape, dt in items:
                made.append(nc.alloc_sbuf_tensor_at(name, [P] + shape, dt, offset=at))
                at += 4 * int(np.prod(shape))
            return at, made

        at, (xt, w_raw, w_hi, w_lo, ident, coef, gate_bias, half_bias, pool_scale,
             nmax, smax, den, rden, stats, mv, rstd, shift_one) = place(base, [
                 ("xt", [KT, 2, SEQ], F32R),
                 ("w_raw", [RING, CHUNK], F32), ("w_hi", [RING, CHUNK], F32R),
                 ("w_lo", [RING, CHUNK], F32R), ("ident", [P], F32),
                 ("coef", [POOL_TILES * POOL_COEFS], F32), ("gate_bias", [2 * OT], F32),
                 ("half_bias", [2 * OT], F32), ("pool_scale", [POOL_TILES], F32),
                 ("nmax", [8], F32), ("smax", [8], F32), ("den", [8], F32), ("rden", [8], F32),
                 ("stats", [TT, BLOCKS, 6], F32), ("mv", [TT, 8], F32), ("rstd", [8], F32),
                 ("shift_one", [TT, 4], F32)])
        at_ya = at
        at, (ya,) = place(at_ya, [("ya", [HEADS, 2, SEQ], F32R)])
        at_p = at
        at, (p_hi, p_lo) = place(at_p, [("p_hi", [POOL_TILES, SEQ], F32R),
                                        ("p_lo", [POOL_TILES, SEQ], F32R)])
        at_szp = at
        at, (szp, corr, gate_f, th_gate, gate, mixed_f, sum_f) = place(at, [
            ("szp", [POOL_TILES, SEQ], F32), ("corr", [2, SEQ], F32), ("gate_f", [2, SEQ], F32),
            ("th_gate", [2, SEQ], F32), ("gate", [2, SEQ], F32), ("mixed_f", [SEQ], F32),
            ("sum_f", [SEQ], F32)])
        at_phase = at
        end_a, (q_hi, q_lo, k_hi, k_lo, v_hi, v_lo, mask, s_sb, pt_hi, pt_lo, silu_za,
                qk_f, u_pad, pool_a, pool_b, inv) = place(at_phase, [
                    ("q_hi", [GROUPS, SEQ], F32R), ("q_lo", [GROUPS, SEQ], F32R),
                    ("k_hi", [GROUPS, SEQ], F32R), ("k_lo", [GROUPS, SEQ], F32R),
                    ("v_hi", [TT, GROUPS * P], F32R),
                    ("v_lo", [TT, GROUPS * P], F32R), ("mask", [S0 + S1], F32),
                    ("s_sb", [S0 + S1], F32), ("pt_hi", [GROUPS, PTW], F32R),
                    ("pt_lo", [GROUPS, PTW], F32R), ("silu_za", [SEQ], F32),
                    ("qk_f", [2, SEQ], F32), ("u_pad", [PAD + SEQ], F32), ("pool_a", [PAD + SEQ], F32),
                    ("pool_b", [PAD + SEQ], F32), ("inv", [POOL_TILES, PAD], F32)])
        _, (xt_raw,) = place(at_phase, [("xt_raw", [KT, SEQ], F32)])
        end_b, (yp, merged) = place(at_phase, [
            ("yp", [POOL_TILES, 2, SEQ], F32R), ("merged", [OT, 2, SEQ], F32R)])
        _, (yp_f,) = place(end_b - 2 * 2 * SEQ * 4, [("yp_f", [2, 2 * SEQ], F32)])
        _, (res,) = place(at_p, [("res", [TT, D_MODEL], F32)])
        _, (gamma, gamma_beta) = place(at_ya, [("gamma", [D_MODEL], F32), ("gamma_beta", [D_MODEL], F32)])
        _, (gb_hi, gb_lo) = place(at_phase, [("gb_hi", [D_MODEL], F32R), ("gb_lo", [D_MODEL], F32R)])
        _, (row_hi, row_lo) = place(at_szp, [("row_hi", [TT, P], F32R), ("row_lo", [TT, P], F32R)])
        _, (corr_pair, pair_f) = place(at_szp, [("corr_pair", [2, SEQ], F32), ("pair_f", [2, SEQ], F32)])
        assert max(end_a, end_b) <= nc.sbuf_usable_end, (end_a, end_b, nc.sbuf_usable_end)

        proj_ps = psum("proj_ps", [P, 2, 512])
        attn_ps = psum("attn_ps", [P, 4 * 512])
        turn_ps = psum("turn_ps", [P, 512])
        mixed_ps = psum("mixed_ps", [P, 512])

        v_ps = (attn_ps[:, 1536:1536 + GROUPS * P], turn_ps[:, 0:GROUPS * P])
        proj_pair = attn_ps[:, 0:1024].rearrange("p (b c) -> p b c", b=2)

        def block_sum(c, t):
            return (turn_ps, mixed_ps)[t] if c % 2 == 0 else attn_ps[:, (2 + t) * 512:(3 + t) * 512]

        def norm_shift(t, c):
            if t == 0:
                return attn_ps[:, c * 512:(c + 1) * 512] if c < 2 else proj_ps[:, c - 2, :]
            return block_sum(c // 2, c % 2)

        x_landed = [sem(f"x_landed{q}") for q in range(4)]
        consts_landed = sem("consts_landed")
        tail_landed = sem("tail_landed")
        first_half_landed = sem("first_half_landed")
        raw_landed = [sem(f"raw_landed{s}") for s in range(RING)]
        x_hi_done = sem("x_hi_done")
        x_lo_done = sem("x_lo_done")
        hi_split = sem("hi_split")
        lo_split = sem("lo_split")
        chunk_done = sem("chunk_done")
        act_evac = sem("act_evac")
        tanh_done = sem("tanh_done")
        proj_free = sem("proj_free")
        bias_ready = sem("bias_ready")
        pads_zero = sem("pads_zero")
        qk_split = sem("qk_split")
        scores_ready = sem("scores_ready")
        max_ready = sem("max_ready")
        exp_done = sem("exp_done")
        probs_ready = sem("probs_ready")
        v_hi_done = sem("v_hi_done")
        v_split = sem("v_split")
        pt_ready = sem("pt_ready")
        pt_hi_done = sem("pt_hi_done")
        pt_split = sem("pt_split")
        mixed_ready = sem("mixed_ready")
        mixed_free = sem("mixed_free")
        y_split = sem("y_split")
        pool_split = sem("pool_split")
        pool_ready = sem("pool_ready")
        yp_f_ready = sem("yp_f_ready")
        yp_hi_done = sem("yp_hi_done")
        yp_split = sem("yp_split")
        merged_split = sem("merged_split")
        first_rows_done = sem("first_rows_done")
        rows_added = sem("rows_added")
        gb_hi_done = sem("gb_hi_done")
        gb_split = sem("gb_split")
        row_turned = sem("row_turned")
        row_hi_done = sem("row_hi_done")
        row_split = sem("row_split")
        norm_shift_ready = sem("norm_shift_ready")
        vec = sem("vec")
        var_ready = sem("var_ready")
        std_ready = sem("std_ready")
        shift_ready = sem("shift_ready")
        out_ready = sem("out_ready")
        out_landed = sem("out_landed")

        N_CONSTS = 6
        CONSTS = 16 * N_CONSTS

        block = ctx.enter_context(nc.Block())

        def landed(eng, n, j, i, per):
            eng.wait_ge(raw_landed[(n + j) % RING], 16 * ((n + j) // RING + 1) + i * (16 * per // RING))

        @block.sync
        def _(sp):
            def load(slot, chunk):
                sp.dma_start(w_raw[:, slot, :], stream_d[chunk, :, :]).then_inc(raw_landed[slot], 16)

            def load_x(q):
                sp.dma_start(xt_raw[:, 4 * q:4 * q + 4, :], xt_d[q, :, :, :]).then_inc(x_landed[q], 16)

            half = HALF * P
            load_x(0)
            sp.dma_start(w_raw[:, 0, 0:half], stream_d[0, :, 0:half]).then_inc(first_half_landed, 16)
            load_x(1)
            sp.dma_start(w_raw[:, 0, half:CHUNK], stream_d[0, :, half:CHUNK]).then_inc(raw_landed[0], 16)
            load_x(2)
            load_x(3)
            load(1, 1)
            load(2, 2)
            whole = (CHUNKS - RING) // RING
            with sp.Fori(0, whole) as i:
                for j in range(RING):
                    sp.wait_ge(lo_split, i * (2 * RING) + 2 * (j + 1))
                    sp.dma_start(w_raw[:, j, :],
                                 stream_d[bass.ds(i * RING + (RING + j), 1), :, :]
                                 .rearrange("a p n -> (a p) n")).then_inc(raw_landed[j], 16)
            for n in range(RING * (whole + 1), CHUNKS):
                sp.wait_ge(lo_split, 2 * (n - RING + 1))
                load(n % RING, n)
            for n in range(TT * BLOCKS):
                sp.wait_ge(out_ready, n + 1)
                t, cols = n // BLOCKS, slice(n % BLOCKS * BLOCK, (n % BLOCKS + 1) * BLOCK)
                sp.dma_start(out_d[t, :, cols], res[:, t, cols]).then_inc(out_landed, 16)
            sp.wait_ge(out_landed, 16 * TT * BLOCKS)

        @block.tensor
        def _(pe):
            mm, turn = nc.tensor.matmul, nc.tensor.transpose

            def product(out, a_hi, a_lo, b_hi, b_lo, first=True, last=True):
                mm(out, a_hi, b_hi, start=first, stop=False)
                mm(out, a_hi, b_lo, start=False, stop=False)
                return mm(out, a_lo, b_hi, start=False, stop=last)

            def chunk(n, j, i, per, moving, between=None):
                slot = (n + j) % RING
                for half in range(2):
                    pe.wait_ge(lo_split, 2 * (n + j) + half + 1 + i * (2 * per))
                    for k in range(half * HALF, (half + 1) * HALF):
                        if between:
                            between(k)
                        bank, tile, first, last = moving(k)
                        cols = slice(k * P, (k + 1) * P)
                        mm(bank, w_hi[:, slot, cols], tile.rearrange("p a s -> p (a s)"),
                           start=first, stop=False)
                        done = mm(bank[:, SEQ:2 * SEQ], w_lo[:, slot, cols], tile[:, 0, :],
                                  start=False, stop=last)
                done.then_inc(chunk_done, 1)

            def next_bank(n, j, i):
                pe.wait_ge(proj_free, FROM + banked(n, j) + i * banked_per(n))

            def from_x(bank):
                return lambda k: (proj_ps[:, bank, :], xt[:, k, :, :], k == 0, k == KT - 1)

            def x_arrives(k):
                if k % 4 == 0:
                    pe.wait_ge(x_lo_done, k // 4 + 1)

            def scores(i):
                pe.wait_ge(qk_split, i * (2 * GROUPS) + 2 * GROUPS)
                pe.wait_ge(pt_split, FROM + i * GROUPS)
                for t in range(TT):
                    for g in range(GROUPS):
                        at = g * P if t == 0 else 512 + g * SEQ
                        keys = (t + 1) * P
                        q = slice(t * P, (t + 1) * P)
                        done = product(attn_ps[:, at:at + keys], q_hi[:, g, q], q_lo[:, g, q],
                                       k_hi[:, g, 0:keys], k_lo[:, g, 0:keys])
                done.then_inc(scores_ready, 1)

            def turn_probs(i):
                pe.wait_ge(consts_landed, CONSTS)
                pe.wait_ge(probs_ready, i * 2 + 2)
                for g in range(GROUPS):
                    at = g * 512
                    turn(attn_ps[:, at:at + P], s_sb[:, g * P:(g + 1) * P], ident[:, :])
                    for kt in range(2):
                        src = S0 + g * SEQ + kt * P
                        done = turn(attn_ps[:, at + P + kt * P:at + 2 * P + kt * P],
                                    s_sb[:, src:src + P], ident[:, :])
                    done.then_inc(pt_ready, 1)

            def values(j, i):
                n = V_FIRST + j
                slot = n % RING
                pe.wait_ge(lo_split, 2 * n + 2 + i * (2 * A_CHUNKS))
                if j == 0:
                    pe.wait_ge(v_split, FROM + i * TT)
                first, end = j * KT, (j + 1) * KT
                for k in range(first // GROUPS, (end - 1) // GROUPS + 1):
                    begin, stop = max(first, k * GROUPS), min(end, (k + 1) * GROUPS)
                    cols = slice((begin - first) * P, (stop - first) * P)
                    out = slice((begin - k * GROUPS) * P, (stop - k * GROUPS) * P)
                    for t in range(TT):
                        tokens = slice(t * P, (t + 1) * P)
                        done = product(v_ps[t][:, out], xt[:, k, 0, tokens], xt[:, k, 1, tokens],
                                       w_hi[:, slot, cols], w_lo[:, slot, cols], k == 0, k == KT - 1)
                done.then_inc(chunk_done, 1)

            def mix(i):
                pe.wait_ge(pt_split, FROM + i * GROUPS + GROUPS)
                pe.wait_ge(v_split, FROM + i * TT + TT)
                pe.wait_ge(mixed_free, FROM + i)
                for g in range(GROUPS):
                    for kt in range(TT):
                        out = mixed_ps[:, 0:SEQ] if kt == 0 else mixed_ps[:, P:SEQ]
                        pcols = slice(0, SEQ) if kt == 0 else slice(SEQ, PTW)
                        v = slice(g * P, (g + 1) * P)
                        done = product(out, v_hi[:, kt, v], v_lo[:, kt, v], pt_hi[:, g, pcols],
                                       pt_lo[:, g, pcols], first=(g == 0 and kt == 0),
                                       last=(g == GROUPS - 1 and kt == TT - 1))
                done.then_inc(mixed_ready, 1)

            pe.sem_inc(chunk_done, FROM)
            with pe.Fori(0, A_STEPS) as i:
                for j in range(A_CHUNKS):
                    if V_FIRST <= j < V_FIRST + GROUPS:
                        values(j - V_FIRST, i)
                    else:
                        chunk(0, j, i, A_CHUNKS, from_x(j % 2), x_arrives if j == 0 else None)
                    next_bank(0, j, i)
                    if j == SCORES_AFTER:
                        scores(i)
                    if j == PT_AFTER:
                        turn_probs(i)
                mix(i)

            pe.wait_ge(lo_split, 2 * POOL_MAP + 2)
            pe.wait_ge(pool_split, POOL_TILES)
            slot = POOL_MAP % RING
            for g in range(POOL_TILES // 2):
                for m in range(2):
                    for kk in range(2):
                        cols = slice((g * 2 + kk) * POOL_GROUP + m * P, (g * 2 + kk) * POOL_GROUP + (m + 1) * P)
                        last = product(attn_ps[:, g * 512 + m * SEQ:g * 512 + (m + 1) * SEQ],
                                       w_hi[:, slot, cols], w_lo[:, slot, cols],
                                       p_hi[:, 2 * g + kk, :], p_lo[:, 2 * g + kk, :],
                                       first=(kk == 0), last=(kk == 1))
                last.then_inc(pool_ready if g < POOL_TILES // 2 - 1 else chunk_done, 1)
            next_bank(B_FIRST, 0, 0)

            def from_y(k):
                bank, kk = k // HALF, k % HALF
                return (attn_ps[:, bank * 512:(bank + 1) * 512], (ya, yp)[bank][:, kk, :, :],
                        kk == 0, kk == HALF - 1)

            with pe.Fori(0, B_STEPS) as i:
                for j in range(B_CHUNKS):
                    bank = (B_FIRST + j) % 2
                    if j % 3 < 2:
                        chunk(B_FIRST, j, i, B_CHUNKS, from_x(bank))
                    else:
                        pe.wait_ge(y_split, HEADS)
                        pe.wait_ge(yp_split, POOL_TILES // 2)
                        chunk(B_FIRST, j, i, B_CHUNKS, from_y)
                    next_bank(B_FIRST, j, i)

            def out_products(n, kk, t):
                c, k = (n - C_FIRST) // BLOCK_CHUNKS, (n - C_FIRST) % BLOCK_CHUNKS * BLOCK_KT + kk
                cols, tokens = slice(kk * BLOCK, (kk + 1) * BLOCK), slice(t * P, (t + 1) * P)
                if k == 0 and c >= 2:
                    pe.wait_ge(rows_added, TT * (c - 2) + t + 1)
                return product(block_sum(c, t)[:, :], merged[:, k, 0, tokens], merged[:, k, 1, tokens],
                               w_hi[:, n % RING, cols], w_lo[:, n % RING, cols], k == 0, k == KT - 1)

            pe.wait_ge(merged_split, OT - 1)
            for n in range(C_FIRST, CHUNKS - 1):
                if n == C_FIRST + BLOCK_CHUNKS - 1:
                    pe.wait_ge(merged_split, OT)
                for kk in range(BLOCK_KT):
                    if kk % 2 == 0:
                        pe.wait_ge(lo_split, 2 * n + kk // 2 + 1)
                    for t in range(TT):
                        done = out_products(n, kk, t)
                done.then_inc(chunk_done, 1)
            pe.wait_ge(lo_split, 2 * CHUNKS)
            for t in range(TT):
                for kk in range(BLOCK_KT):
                    done = out_products(CHUNKS - 1, kk, t)
                done.then_inc((first_rows_done, chunk_done)[t], 1)

            def turn_row(t):
                pe.wait_ge(shift_ready, t + 1)
                turn((turn_ps, mixed_ps)[t][0:2, 0:P], shift_one[:, t, 0:2], ident[:, :]).then_inc(row_turned, 1)

            def shift_product(t, c):
                cols = slice(c * BLOCK, (c + 1) * BLOCK)
                product(norm_shift(t, c)[:, :], row_hi[0:2, t, :], row_lo[0:2, t, :],
                        gb_hi[0:2, cols], gb_lo[0:2, cols]).then_inc(norm_shift_ready, 1)

            turn_row(0)
            pe.wait_ge(gb_split, 1)
            pe.wait_ge(row_split, 1)
            for c in range(BLOCKS):
                if c == BLOCKS - 1:
                    turn_row(1)
                shift_product(0, c)
            pe.wait_ge(row_split, 2)
            pe.wait_ge(rows_added, TT * BLOCKS)
            for c in range(BLOCKS):
                shift_product(1, c)

        @block.scalar
        def _(act):
            activation = nc.scalar.activation

            def hi_part(slot, half):
                cols = slice(half * HALF * P, (half + 1) * HALF * P)
                activation(w_hi[:, slot, cols], w_raw[:, slot, cols], ACT.Copy).then_inc(hi_split, 1)

            def split_hi(n, j, i, per):
                landed(act, n, j, i, per)
                if n or j >= RING or per:
                    act.wait_ge(chunk_done, FROM + n + j - AHEAD + i * per)
                for half in range(2):
                    hi_part((n + j) % RING, half)

            def correction(n, j, i, per, pair=False):
                act.wait_ge(chunk_done, FROM + n + j + 1 + i * per)
                if pair:
                    act.wait_ge(proj_free, FROM + banked(n, j) - 2 + i * banked_per(n))
                    activation(corr_pair[:, :, :], proj_pair[:, :, SEQ:2 * SEQ], ACT.Copy).then_inc(act_evac, 1)
                else:
                    b = (n + j) % 2
                    activation(corr[:, b, :], proj_ps[:, b, SEQ:2 * SEQ], ACT.Copy).then_inc(act_evac, 1)
                act.wait_ge(proj_free, FROM + banked(n, j) + i * banked_per(n))

            for q in range(4):
                act.wait_ge(x_landed[q], 16)
                activation(xt[:, 4 * q:4 * q + 4, 0, :], xt_raw[:, 4 * q:4 * q + 4, :],
                           ACT.Copy).then_inc(x_hi_done, 1)
                if q < 2:
                    act.wait_ge((first_half_landed, raw_landed[0])[q], 16)
                    hi_part(0, q)
            for dst, src in ((ident[:, :], ident_d), (coef[:, :], coef_d), (gate_bias[:, :], bias_d),
                             (pool_scale[:, :], scale_d), (mask[:, :], mask_d), (inv[:, :, :], inv_d)):
                act.dma_start(dst, src).then_inc(consts_landed, 16)
            split_hi(0, 1, 0, 0)

            def exp_probs(i):
                act.wait_ge(max_ready, i + 1)
                for t, cols in ((0, slice(0, S0)), (1, slice(S0, S0 + S1))):
                    activation(s_sb[:, cols], s_sb[:, cols], ACT.Exp, bias=nmax[:, t:t + 1], scale=SCALE,
                               accum_out=den[:, t:t + 1]).then_inc(exp_done, 1)

            def v_hi_parts(i):
                act.wait_ge(chunk_done, FROM + V_FIRST + GROUPS + i * A_CHUNKS)
                for t in range(TT):
                    activation(v_hi[:, t, :], v_ps[t][:, :], ACT.Copy).then_inc(v_hi_done, 1)

            with act.Fori(0, A_STEPS) as i:
                for j in range(A_CHUNKS):
                    if j == V_FIRST:
                        exp_probs(i)
                    if j == V_FIRST + 2:
                        for g in range(GROUPS):
                            act.wait_ge(pt_ready, i * GROUPS + g + 1)
                            activation(pt_hi[:, g, :], attn_ps[:, g * 512:g * 512 + PTW],
                                       ACT.Copy).then_inc(pt_hi_done, 1)
                    split_hi(0, j + AHEAD, i, A_CHUNKS)
                    if j == V_FIRST + GROUPS - 1:
                        v_hi_parts(i)
                    if not V_FIRST <= j < V_FIRST + GROUPS:
                        correction(0, j, i, A_CHUNKS)
                    if j in (Z_ATTN, Z_POOL):
                        act.wait_ge(proj_free, FROM + banked(0, j) + 1 + i * A_BANKED)
                        z = int(j == Z_POOL)
                        activation(th_gate[:, z, :], gate_f[:, z, :], ACT.Tanh, scale=0.5).then_inc(tanh_done, 1)

            split_hi(POOL_MAP, AHEAD, 0, 0)
            act.wait_ge(chunk_done, FROM + POOL_MAP + 1)
            act.dma_start(res[:, :, :], x_d).then_inc(tail_landed, 16)
            for g in range(POOL_TILES // 2):
                act.wait_ge(yp_f_ready, g + 1)
                activation(yp[:, 2 * g:2 * g + 2, 0, :],
                           yp_f[:, g % 2, :].rearrange("p (m s) -> p m s", m=2), ACT.Copy).then_inc(yp_hi_done, 1)
            act.wait_ge(bias_ready, 1)
            with act.Fori(0, B_STEPS) as i:
                for j in range(B_CHUNKS):
                    split_hi(B_FIRST, j + AHEAD, i, B_CHUNKS)
                    correction(B_FIRST, j, i, B_CHUNKS, pair=j % 3 == 2)
                    if j % 3 < 2:
                        act.wait_ge(proj_free, FROM + banked(B_FIRST, j) + 1 + i * B_CHUNKS)
                        activation(th_gate[:, j % 3, :], gate_f[:, j % 3, :], ACT.Tanh,
                                   bias=half_bias[:, bass.ds(i * 4 + ((j % 3) * OT + j // 3), 1)],
                                   scale=0.5).then_inc(tanh_done, 1)
            act.wait_ge(chunk_done, FROM + C_FIRST)
            act.dma_start(gamma[:, :], gamma_d).then_inc(tail_landed, 16)
            act.dma_start(gamma_beta[0:2, :], gamma_beta_d).then_inc(tail_landed, 16)
            whole = (OT - AHEAD) // RING
            with act.Fori(0, whole) as i:
                for j in range(RING):
                    split_hi(C_FIRST, j + AHEAD, i, RING)
            for e in range(whole * RING + AHEAD, OT):
                split_hi(C_FIRST, e, 0, 0)
            act.wait_ge(tail_landed, 16 * 3)
            activation(gb_hi[0:2, :], gamma_beta[0:2, :], ACT.Copy).then_inc(gb_hi_done, 1)
            activation(rstd[:, 4:5], ident[:, 0:1], ACT.Sqrt)
            for t in range(TT):
                act.wait_ge(var_ready, t + 1)
                activation(rstd[:, t:t + 1], mv[:, t, 2:3], ACT.Sqrt).then_inc(std_ready, 1)
                act.wait_ge(row_turned, t + 1)
                activation(row_hi[0:2, t, :], (turn_ps, mixed_ps)[t][0:2, 0:P], ACT.Copy).then_inc(row_hi_done, 1)

        @block.vector
        def _(dve):
            tt, ts = nc.vector.tensor_tensor, nc.vector.tensor_scalar
            stt, copy = nc.vector.scalar_tensor_tensor, nc.vector.tensor_copy

            class Chain:
                count, per, i = 0, 0, 0

                def ready(self):
                    dve.wait_ge(vec, self.count + (self.i * self.per if self.per else 0))

                def add(self, ins):
                    ins.then_inc(vec, 1)
                    self.count += 1

                def link(self, ins):
                    self.add(ins)
                    self.ready()

            chain = Chain()
            for counted in (proj_free, pt_split, v_split, mixed_free):
                dve.sem_inc(counted, FROM)

            def lo_part(slot, half):
                cols = slice(half * HALF * P, (half + 1) * HALF * P)
                tt(w_lo[:, slot, cols], w_raw[:, slot, cols], w_hi[:, slot, cols].bitcast(F32),
                   ALU.subtract).then_inc(lo_split, 1)

            def split_lo(n, j, i, per):
                slot = (n + j) % RING
                for half in range(2):
                    dve.wait_ge(hi_split, 2 * (n + j) + half + 1 + i * (2 * per))
                    lo_part(slot, half)

            def halves_summed(dst, n, j, i):
                dve.wait_ge(act_evac, banked(n, j) + 1 + i * banked_per(n))
                tt(dst, proj_ps[:, (n + j) % 2, 0:SEQ], corr[:, (n + j) % 2, :], ALU.add).then_inc(proj_free, 1)

            def freed(n, j, i):
                dve.wait_ge(proj_free, FROM + banked(n, j) + 1 + i * banked_per(n))

            for q in range(4):
                dve.wait_ge(x_hi_done, q + 1)
                tt(xt[:, 4 * q:4 * q + 4, 1, :], xt_raw[:, 4 * q:4 * q + 4, :],
                   xt[:, 4 * q:4 * q + 4, 0, :].bitcast(F32), ALU.subtract).then_inc(x_lo_done, 1)
                if q < 2:
                    dve.wait_ge(hi_split, q + 1)
                    lo_part(0, q)
            for pad in (u_pad, pool_a, pool_b):
                chain.link(nc.vector.memset(pad[:, 0:PAD], 0.0))
            split_lo(0, 1, 0, 0)

            def sigmoid(z, count, i, per):
                dve.wait_ge(tanh_done, count + i * per)
                chain.link(ts(gate[:, z, :], th_gate[:, z, :], 0.5, 0.5, ALU.mult, ALU.add))

            def masked_max(i):
                dve.wait_ge(scores_ready, i + 1)
                dve.wait_ge(consts_landed, CONSTS)
                chain.add(nc.vector.memset(smax[:, 4:6], 0.0))
                for t, at, cols in ((0, 0, slice(0, S0)), (1, 512, slice(S0, S0 + S1))):
                    chain.add(nc.vector.tensor_tensor_reduce(
                        s_sb[:, cols], attn_ps[:, at:at + cols.stop - cols.start], mask[:, cols], 1.0,
                        -3.0e38, ALU.add, ALU.max, smax[:, t:t + 1]))
                chain.ready()
                ts(nmax[:, 0:2], smax[:, 0:2], -SCALE, None, ALU.mult).then_inc(max_ready, 1)

            def normalise(i):
                dve.wait_ge(exp_done, i * 2 + 2)
                chain.link(nc.vector.reciprocal(rden[:, 0:2], den[:, 0:2]))
                for t, cols in ((0, slice(0, S0)), (1, slice(S0, S0 + S1))):
                    ts(s_sb[:, cols], s_sb[:, cols], rden[:, t:t + 1], None, ALU.mult).then_inc(probs_ready, 1)

            def pool(h):
                src = u_pad
                for k, dst in enumerate((pool_a, pool_b, pool_a, pool_b)):
                    back = PAD - 2 ** k
                    chain.link(stt(out=dst[:, PAD:PAD + SEQ], in0=src[:, back:back + SEQ],
                                   scalar=coef[:, bass.ds(h * POOL_COEFS + k, 1)],
                                   in1=src[:, PAD:PAD + SEQ], op0=ALU.mult, op1=ALU.add))
                    src = dst
                chain.link(tt(pool_a[:, PAD:2 * PAD], src[:, PAD:2 * PAD], tile_of(inv, h), ALU.mult))
                chain.add(tt(sum_f[:, 0:PAD], pool_a[:, PAD:2 * PAD], u_pad[:, PAD:2 * PAD], ALU.subtract))
                chain.link(stt(out=sum_f[:, PAD:SEQ], in0=src[:, 2 * PAD:PAD + SEQ],
                               scalar=coef[:, bass.ds(h * POOL_COEFS + POOL_STEPS, 1)],
                               in1=u_pad[:, 2 * PAD:PAD + SEQ], op0=ALU.mult, op1=ALU.subtract))
                chain.link(copy(tile_of(p_hi, h), sum_f[:, :]))
                tt(tile_of(p_lo, h), sum_f[:, :], tile_of(p_hi, h).bitcast(F32), ALU.subtract).then_inc(pool_split, 1)

            def tile_of(t, tile):
                return t[:, bass.ds(tile, 1), :].rearrange("p a s -> p (a s)")

            def split(src, parts, tile, signal):
                both = parts[:, bass.ds(tile, 1), :, :].rearrange("p a b s -> p (a b) s")
                chain.link(copy(both[:, 0, :], src))
                tt(both[:, 1, :], src, both[:, 0, :].bitcast(F32), ALU.subtract).then_inc(signal, 1)

            per_a = 23
            start_a = chain.count
            with dve.Fori(0, A_STEPS) as i:
                chain.i, chain.per = i, per_a
                for j in range(A_CHUNKS):
                    if j == V_FIRST:
                        normalise(i)
                    if j == V_FIRST + 2:
                        for g in range(GROUPS):
                            dve.wait_ge(pt_hi_done, i * GROUPS + g + 1)
                            tt(pt_lo[:, g, :], attn_ps[:, g * 512:g * 512 + PTW],
                               pt_hi[:, g, :].bitcast(F32), ALU.subtract).then_inc(pt_split, 1)
                    if j == Z_POOL:
                        freed(0, U_POOL, i)
                        pool(i)
                    split_lo(0, j + AHEAD, i, A_CHUNKS)
                    if j < Z_ATTN:
                        hi, lo = ((q_hi, q_lo), (k_hi, k_lo))[j % 2]
                        g = j // 2
                        halves_summed(qk_f[:, j % 2, :], 0, j, i)
                        freed(0, j, i)
                        chain.link(copy(hi[:, g, :], qk_f[:, j % 2, :]))
                        tt(lo[:, g, :], qk_f[:, j % 2, :], hi[:, g, :].bitcast(F32),
                           ALU.subtract).then_inc(qk_split, 1)
                    if j == Z_ATTN:
                        halves_summed(gate_f[:, 0, :], 0, j, i)
                        masked_max(i)
                        sigmoid(0, 1, i, 2)
                        chain.add(tt(silu_za[:, :], gate_f[:, 0, :], gate[:, 0, :], ALU.mult))
                    if j == V_FIRST + GROUPS - 1:
                        for t in range(TT):
                            dve.wait_ge(v_hi_done, i * TT + t + 1)
                            tt(v_lo[:, t, :], v_ps[t][:, :], v_hi[:, t, :].bitcast(F32),
                               ALU.subtract).then_inc(v_split, 1)
                    if j == U_POOL:
                        halves_summed(u_pad[:, PAD:PAD + SEQ], 0, j, i)
                    if j == Z_POOL:
                        halves_summed(gate_f[:, 1, :], 0, j, i)
                        sigmoid(1, 2, i, 2)
                        chain.add(stt(out=tile_of(szp, i), in0=gate_f[:, 1, :],
                                      scalar=pool_scale[:, bass.ds(i, 1)], in1=gate[:, 1, :],
                                      op0=ALU.mult, op1=ALU.mult))
                dve.wait_ge(mixed_ready, i + 1)
                tt(mixed_f[:, :], mixed_ps[:, 0:SEQ], silu_za[:, :], ALU.mult).then_inc(mixed_free, 1)
                dve.wait_ge(mixed_free, FROM + i + 1)
                split(mixed_f[:, :], ya, i, y_split)
            assert chain.count - start_a == per_a, chain.count - start_a
            chain.count, chain.per = start_a + per_a * A_STEPS, 0

            split_lo(POOL_MAP, AHEAD, 0, 0)
            ts(half_bias[:, :], gate_bias[:, :], 0.5, None, ALU.mult).then_inc(bias_ready, 1)
            for g in range(POOL_TILES // 2):
                if g < POOL_TILES // 2 - 1:
                    dve.wait_ge(pool_ready, g + 1)
                else:
                    dve.wait_ge(chunk_done, FROM + POOL_MAP + 1)
                if g >= 2:
                    dve.wait_ge(yp_split, g - 1)
                tt(yp_f[:, g % 2, :], attn_ps[:, g * 512:(g + 1) * 512],
                   szp[:, 2 * g:2 * g + 2, :].rearrange("p a s -> p (a s)"), ALU.mult).then_inc(yp_f_ready, 1)
                if g % 2 == 1:
                    for b in (g - 1, g):
                        dve.wait_ge(yp_hi_done, b + 1)
                        tt(yp[:, 2 * b:2 * b + 2, 1, :], yp_f[:, b % 2, :].rearrange("p (m s) -> p m s", m=2),
                           yp[:, 2 * b:2 * b + 2, 0, :].bitcast(F32), ALU.subtract).then_inc(yp_split, 1)

            per_b = 4 * 5
            start_b = chain.count
            with dve.Fori(0, B_STEPS) as i:
                chain.i, chain.per = i, per_b
                for j in range(B_CHUNKS):
                    split_lo(B_FIRST, j + AHEAD, i, B_CHUNKS)
                    tanhs = 2 * A_STEPS + j // 3 * 2
                    if j % 3 < 2:
                        if j % 3 == 1:
                            sigmoid(0, tanhs + 1, i, 2 * B_STEPS)
                        halves_summed(gate_f[:, j % 3, :], B_FIRST, j, i)
                    else:
                        sigmoid(1, tanhs + 2, i, 2 * B_STEPS)
                        dve.wait_ge(act_evac, banked(B_FIRST, j) + 1 + i * B_CHUNKS)
                        tt(pair_f[:, :, :], proj_pair[:, :, 0:SEQ], corr_pair[:, :, :],
                           ALU.add).then_inc(proj_free, 1)
                        freed(B_FIRST, j, i)
                        chain.link(tt(pair_f[:, :, :], pair_f[:, :, :], gate[:, :, :], ALU.mult))
                        chain.link(tt(sum_f[:, :], pair_f[:, 0, :], pair_f[:, 1, :], ALU.add))
                        split(sum_f[:, :], merged, i * 4 + j // 3, merged_split)
            assert chain.count - start_b == per_b, chain.count - start_b
            chain.count, chain.per = start_b + per_b * B_STEPS, 0

            def add_rows(c, t):
                at = res[:, t, c * BLOCK:(c + 1) * BLOCK]
                stt(out=at, in0=at, scalar=ALPHA, in1=block_sum(c, t)[:, :],
                    op0=ALU.mult, op1=ALU.add).then_inc(rows_added, 1)

            def statistics(c, t):
                dve.wait_ge(rows_added, TT * c + t + 1)
                chain.add(nc.vector.bn_stats(stats[:, t, c, :], res[:, t, c * BLOCK:(c + 1) * BLOCK]))

            def times_gamma(c, t):
                at = res[:, t, c * BLOCK:(c + 1) * BLOCK]
                chain.add(tt(at, at, gamma[:, c * BLOCK:(c + 1) * BLOCK], ALU.mult))

            def variance(t):
                chain.ready()
                chain.link(nc.vector.bn_aggr(mv[:, t, 0:2], stats[:, t, :, :].rearrange("p a s -> p (a s)")))
                ts(mv[:, t, 2:3], mv[:, t, 1:2], LN_EPS, None, ALU.add).then_inc(var_ready, 1)

            def token_shift(t):
                dve.wait_ge(std_ready, t + 1)
                chain.link(nc.vector.reciprocal(rstd[:, 2 + t:3 + t], rstd[:, t:t + 1]))
                stt(out=shift_one[:, t, 0:1], in0=mv[:, t, 0:1], scalar=-1.0, in1=rstd[:, 2 + t:3 + t],
                    op0=ALU.mult, op1=ALU.mult).then_inc(shift_ready, 1)

            def row_lo_part(t):
                dve.wait_ge(row_hi_done, t + 1)
                tt(row_lo[0:2, t, :], (turn_ps, mixed_ps)[t][0:2, 0:P], row_hi[0:2, t, :].bitcast(F32),
                   ALU.subtract).then_inc(row_split, 1)

            def normalise_rows(t, c):
                dve.wait_ge(norm_shift_ready, t * BLOCKS + c + 1)
                at = res[:, t, c * BLOCK:(c + 1) * BLOCK]
                stt(out=at, in0=at, scalar=rstd[:, 2 + t:3 + t], in1=norm_shift(t, c)[:, :],
                    op0=ALU.mult, op1=ALU.add).then_inc(out_ready, 1)

            chain.link(nc.vector.memset(shift_one[:, :, :], 1.0))
            for e in range(OT - 1):
                if e + AHEAD < OT:
                    split_lo(C_FIRST, e + AHEAD, 0, 0)
                if e % BLOCK_CHUNKS == BLOCK_CHUNKS - 1:
                    c = e // BLOCK_CHUNKS
                    dve.wait_ge(chunk_done, FROM + C_FIRST + e + 1)
                    dve.wait_ge(tail_landed, 16 * 3)
                    for t in range(TT):
                        add_rows(c, t)
                    for t in range(TT):
                        statistics(c, t)
                    chain.ready()
                    for t in range(TT):
                        times_gamma(c, t)
            dve.wait_ge(gb_hi_done, 1)
            tt(gb_lo[0:2, :], gamma_beta[0:2, :], gb_hi[0:2, :].bitcast(F32), ALU.subtract).then_inc(gb_split, 1)
            c = BLOCKS - 1
            dve.wait_ge(first_rows_done, 1)
            add_rows(c, 0)
            statistics(c, 0)
            variance(0)
            times_gamma(c, 0)
            token_shift(0)
            dve.wait_ge(chunk_done, FROM + CHUNKS)
            add_rows(c, 1)
            statistics(c, 1)
            variance(1)
            row_lo_part(0)
            times_gamma(c, 1)
            token_shift(1)
            for b in range(BLOCKS):
                normalise_rows(0, b)
                if b == 0:
                    row_lo_part(1)
            for b in range(BLOCKS):
                normalise_rows(1, b)


def _mask():
    t, s = np.arange(SEQ)[:, None], np.arange(SEQ)[None, :]
    tiles = []
    for tile in range(TT):
        for window, dilation in DILATED:
            sees = (s <= t) & (t - s <= window) & ((t - s) % dilation == 0)
            m = np.where(sees, 0.0, NEG_INF).astype(np.float32)
            tiles.append(m[tile * P:(tile + 1) * P, :(tile + 1) * P])
    return np.ascontiguousarray(np.concatenate(tiles, axis=1))


def _pool_tables():
    coef = np.zeros((POOL_TILES, POOL_COEFS), np.float32)
    inv = np.zeros((POOL_TILES, PAD), np.float32)
    for tile in range(POOL_TILES):
        w = POOL_WINDOWS[tile * P // POOL_GROUP]
        coef[tile, :int(np.log2(w))] = 1.0
        coef[tile, POOL_STEPS] = 1.0 / w
        inv[tile] = 1.0 / np.minimum(np.arange(1, PAD + 1), w).astype(np.float32)
    return (np.ascontiguousarray(np.broadcast_to(coef.reshape(1, -1), (P, POOL_TILES * POOL_COEFS))),
            np.ascontiguousarray(np.broadcast_to(inv.reshape(1, POOL_TILES, PAD), (P, POOL_TILES, PAD))))


def _tiles(w):
    k, n = w.shape
    return w.reshape(k // P, P, n // P, P).transpose(2, 1, 0, 3)


def _stream(w_in, w_pool, w_proj_attn, w_proj_pool, w_out):
    cols = _tiles(w_in)
    qkv = GROUPS * HEADS
    z_attn, u_pool, z_pool = 3 * qkv, 3 * qkv + HEADS, 3 * qkv + HEADS + POOL_TILES
    gates = z_pool + POOL_TILES
    stream = np.empty((CHUNKS, P, CHUNK), np.float32)
    n = 0
    for h in range(HEADS):
        order = [part * qkv + g * HEADS + h for g in range(GROUPS) for part in range(2)]
        order += [z_attn + h] + [None] * GROUPS + [u_pool + h, z_pool + h]
        for j, tile in enumerate(order):
            if tile is not None:
                stream[n + j] = cols[tile].reshape(P, CHUNK)
        values = cols[2 * qkv + h:3 * qkv:HEADS].transpose(1, 2, 0, 3).reshape(P, GROUPS, CHUNK)
        stream[n + V_FIRST:n + V_FIRST + GROUPS] = values.transpose(1, 0, 2)
        n += A_CHUNKS
    stream[n] = w_pool.reshape(4, 2, P, POOL_GROUP).transpose(2, 0, 1, 3).reshape(P, CHUNK)
    n += 1
    attn, pool = _tiles(w_proj_attn), _tiles(w_proj_pool)
    last = w_out.reshape(BLOCK_CHUNKS, BLOCK_KT, P, BLOCKS, BLOCK).transpose(3, 0, 2, 1, 4)
    for d in range(OT):
        stream[n] = cols[gates + d].reshape(P, CHUNK)
        stream[n + 1] = cols[gates + OT + d].reshape(P, CHUNK)
        stream[n + 2] = np.concatenate([attn[d], pool[d]], axis=1).reshape(P, CHUNK)
        n += 3
    stream[n:] = last.reshape(OT, P, CHUNK)
    return stream


def kernel(x, w_in, b_gate, w_pool, pool_scale, w_proj_attn, w_proj_pool, w_out, ln_gamma, ln_beta):
    import concourse.bacc as bacc
    from concourse.bass_utils import run_bass_kernel_spmd

    x = np.asarray(x)[0]
    w_in, b_gate, w_pool, pool_scale, w_proj_attn, w_proj_pool, w_out, ln_gamma, ln_beta = (
        np.asarray(a)[0] for a in (w_in, b_gate, w_pool, pool_scale, w_proj_attn, w_proj_pool, w_out,
                                   ln_gamma, ln_beta))
    coef, inv = _pool_tables()
    arrays = {
        "xt": x.T.reshape(4, 4, P, SEQ).transpose(0, 2, 1, 3),
        "x_rows": x.reshape(TT, P, D_MODEL).transpose(1, 0, 2),
        "weights": _stream(w_in, w_pool, w_proj_attn, w_proj_pool, w_out),
        "gate_bias": b_gate.reshape(2 * OT, P).T,
        "pool_scale": pool_scale.reshape(POOL_TILES, P).T,
        "gamma_row": ln_gamma.reshape(1, D_MODEL).repeat(P, axis=0),
        "gamma_beta": np.stack([ln_gamma, ln_beta]),
        "identity": np.eye(P, dtype=np.float32),
        "mask": _mask(),
        "pool_coef": coef,
        "pool_inv": inv,
    }
    arrays = {f"in_{k}": np.ascontiguousarray(v) for k, v in arrays.items()}
    nc = bacc.Bacc("TRN2", target_bir_lowering=False, num_devices=1)
    args = [nc.dram_tensor(k, v.shape, mybir.dt.from_np(v.dtype), kind="ExternalInput").ap()
            for k, v in arrays.items()]
    args.append(nc.dram_tensor("out_rows", (TT, P, D_MODEL), F32, kind="ExternalOutput").ap())
    layer_kernel(nc, *args)
    r = run_bass_kernel_spmd(nc, [arrays], core_ids=[0])
    return r.results[0]["out_rows"].reshape(1, SEQ, D_MODEL)
```

```python
from contextlib import ExitStack

import numpy as np

import concourse.bass as bass
from concourse import mybir

F32 = mybir.dt.float32
F32R = mybir.dt.float32r
ALU = mybir.AluOpType
ACT = mybir.ActivationFunctionType

P = 128
SEQ = 256
D_MODEL = 2048
HEADS = 8
HEAD_DIM = 128
DILATED = ((128, 1), (512, 4), (2048, 16))
GROUPS = len(DILATED)
POOL_WINDOWS = (2, 4, 8, 16)
POOL_GROUP = 256
POOL_WIDTH = D_MODEL // 2
POOL_TILES = POOL_WIDTH // P
POOL_STEPS = 4
POOL_COEFS = POOL_STEPS + 1
LN_EPS = 1e-5
ALPHA = 2.0 ** 0.25
SCALE = HEAD_DIM ** -0.5
NEG_INF = -1e30

TT = SEQ // P
KT = D_MODEL // P
OT = D_MODEL // P
HALF = KT // 2
CHUNK = KT * P
RING = 3
AHEAD = 2
WARM_UP = 17

A_STEPS, A_CHUNKS = HEADS, 12
B_STEPS, B_CHUNKS = 4, 12
A_BANKED = A_CHUNKS - GROUPS
POOL_MAP = A_STEPS * A_CHUNKS
B_FIRST = POOL_MAP + 1
C_FIRST = B_FIRST + B_STEPS * B_CHUNKS
CHUNKS = C_FIRST + OT
BLOCK = 512
ROWS = 5
BLOCKS = D_MODEL // BLOCK
BLOCK_CHUNKS = OT // BLOCKS
BLOCK_KT = KT // BLOCK_CHUNKS
FROM = 1

V_FIRST, Z_ATTN, U_POOL, Z_POOL = 6, 9, 10, 11
SCORES_AFTER, SOFTMAX_SUM, PT_AFTER, PT_SPLIT = 6, 7, 8, 9
assert V_FIRST % RING == 0 and GROUPS == RING
S0 = GROUPS * P
THIRD = 512 + GROUPS * SEQ
S1 = GROUPS * SEQ
PTW = SEQ + P
PAD = 16


def banked(n, j):
    if n == 0:
        return j - min(max(j - V_FIRST, 0), GROUPS)
    return A_STEPS * A_BANKED + n - B_FIRST + j


def banked_per(n):
    return A_BANKED if n == 0 else B_CHUNKS


def layer_kernel(nc, xt_d, x_d, stream_d, bias_d, scale_d, gamma_d, rows_d, row_kind_d, ident_d, mask_d,
                 coef_d, inv_d, out_d):
    with ExitStack() as ctx:
        def sem(name):
            return ctx.enter_context(nc.semaphore(name))

        def psum(name, shape):
            return ctx.enter_context(nc.psum_tensor(name, shape, F32))

        arena = ctx.enter_context(nc.sbuf_tensor("arena", [P, 206 * 256], F32))
        del arena
        base = nc.sbuf_base - 206 * 1024
        base = (base + 31) // 32 * 32

        def place(at, items):
            made = []
            for name, shape, dt in items:
                made.append(nc.alloc_sbuf_tensor_at(name, [P] + shape, dt, offset=at))
                at += 4 * int(np.prod(shape))
            return at, made

        at, (xt, w_raw, w_hi, w_lo, ident, coef, gate_bias, half_bias, pool_scale,
             nmax, smax, den, rden, stats, mv, rstd, shift_parts, shift,
             row_kind) = place(base, [
                 ("xt", [KT, 2, SEQ], F32R),
                 ("w_raw", [RING, CHUNK], F32), ("w_hi", [RING, CHUNK], F32R),
                 ("w_lo", [RING, CHUNK], F32R), ("ident", [P], F32),
                 ("coef", [POOL_TILES * POOL_COEFS], F32), ("gate_bias", [2 * OT], F32),
                 ("half_bias", [2 * OT], F32), ("pool_scale", [POOL_TILES], F32),
                 ("nmax", [8], F32), ("smax", [8], F32), ("den", [8], F32), ("rden", [8], F32),
                 ("stats", [TT, BLOCKS, 6], F32), ("mv", [TT, 8], F32), ("rstd", [8], F32),
                 ("shift_parts", [TT, 8], F32), ("shift", [8], F32),
                 ("row_kind", [8], F32)])
        at_ya = at
        at, (ya,) = place(at_ya, [("ya", [HEADS, 2, SEQ], F32R)])
        at_p = at
        at, (p_hi, p_lo) = place(at_p, [("p_hi", [POOL_TILES, SEQ], F32R),
                                        ("p_lo", [POOL_TILES, SEQ], F32R)])
        at_szp = at
        at, (szp, corr, gate_f, th_gate, gate, mixed_f, sum_f) = place(at, [
            ("szp", [POOL_TILES, SEQ], F32), ("corr", [2, SEQ], F32), ("gate_f", [2, SEQ], F32),
            ("th_gate", [2, SEQ], F32), ("gate", [2, SEQ], F32), ("mixed_f", [SEQ], F32),
            ("sum_f", [SEQ], F32)])
        at_phase = at
        end_a, (q_hi, q_lo, keys, v_hi, v_lo, mask, s_sb, pt, mixed_corr, silu_za,
                qk_f, u_pad, pool_a, pool_b, inv) = place(at_phase, [
                    ("q_hi", [GROUPS, SEQ], F32R), ("q_lo", [GROUPS, SEQ], F32R),
                    ("keys", [GROUPS, 2, SEQ], F32R),
                    ("v_hi", [TT, GROUPS * P], F32R),
                    ("v_lo", [TT, GROUPS * P], F32R), ("mask", [S0 + S1], F32),
                    ("s_sb", [S0 + S1], F32), ("pt", [GROUPS, 2, PTW], F32R),
                    ("mixed_corr", [SEQ], F32), ("silu_za", [SEQ], F32),
                    ("qk_f", [2, SEQ], F32), ("u_pad", [PAD + SEQ], F32), ("pool_a", [PAD + SEQ], F32),
                    ("pool_b", [PAD + SEQ], F32), ("inv", [POOL_TILES, PAD], F32)])
        _, (xt_raw,) = place(at_phase, [("xt_raw", [KT, SEQ], F32)])
        _, (zeros,) = place(at_ya, [("zeros", [512], F32R)])
        end_b, (yp, merged) = place(at_phase, [
            ("yp", [POOL_TILES, 2, SEQ], F32R), ("merged", [OT, 2, SEQ], F32R)])
        _, (yp_f,) = place(end_b - 2 * 2 * SEQ * 4, [("yp_f", [2, 2 * SEQ], F32)])
        _, (res,) = place(at_p, [("res", [TT, D_MODEL], F32)])
        _, (gamma, rows) = place(at_ya, [("gamma", [D_MODEL], F32), ("rows", [D_MODEL], F32)])
        _, (rows_hi, rows_signed) = place(at_phase, [
            ("rows_hi", [D_MODEL], F32), ("rows_signed", [D_MODEL], F32)])
        _, (shift_rows, row_parts) = place(at_szp, [
            ("shift_rows", [TT, P], F32R), ("row_parts", [D_MODEL], F32R)])
        _, (corr_pair, pair_f) = place(at_szp, [("corr_pair", [2, SEQ], F32), ("pair_f", [2, SEQ], F32)])
        assert max(end_a, end_b) <= nc.sbuf_usable_end, (end_a, end_b, nc.sbuf_usable_end)

        proj_ps = psum("proj_ps", [P, 2, 512])
        attn_ps = psum("attn_ps", [P, 4 * 512])
        value_ps = psum("value_ps", [P, 512])
        mixed_ps = psum("mixed_ps", [P, 512])

        v_ps = (attn_ps[:, 1536:1536 + GROUPS * P], value_ps[:, 0:GROUPS * P])
        proj_pair = attn_ps[:, 0:1024].rearrange("p (b c) -> p b c", b=2)

        def block_sum(c, t):
            return (value_ps, mixed_ps)[t] if c % 2 == 0 else attn_ps[:, (2 + t) * 512:(3 + t) * 512]

        def norm_shift(t, c):
            if t == 0:
                return attn_ps[:, c * 512:(c + 1) * 512] if c < 2 else proj_ps[:, c - 2, :]
            return block_sum(c // 2, c % 2)

        x_landed = [sem(f"x_landed{q}") for q in range(4)]
        consts_landed = sem("consts_landed")
        tail_landed = sem("tail_landed")
        first_half_landed = [sem(f"first_half_landed{n}") for n in range(2)]
        raw_landed = [sem(f"raw_landed{s}") for s in range(RING)]
        zeros_ready = sem("zeros_ready")
        x_hi_done = sem("x_hi_done")
        x_lo_done = sem("x_lo_done")
        hi_split = sem("hi_split")
        lo_split = sem("lo_split")
        chunk_done = sem("chunk_done")
        act_evac = sem("act_evac")
        tanh_done = sem("tanh_done")
        proj_free = sem("proj_free")
        bias_ready = sem("bias_ready")
        qk_split = sem("qk_split")
        scores_ready = sem("scores_ready")
        max_ready = sem("max_ready")
        exp_done = sem("exp_done")
        probs_ready = sem("probs_ready")
        v_hi_done = sem("v_hi_done")
        v_split = sem("v_split")
        pt_ready = sem("pt_ready")
        pt_hi_done = sem("pt_hi_done")
        pt_split = sem("pt_split")
        mixed_ready = sem("mixed_ready")
        mixed_corr_done = sem("mixed_corr_done")
        mixed_free = sem("mixed_free")
        y_split = sem("y_split")
        pool_split = sem("pool_split")
        pool_ready = sem("pool_ready")
        yp_f_ready = sem("yp_f_ready")
        yp_hi_done = sem("yp_hi_done")
        yp_split = sem("yp_split")
        merged_split = sem("merged_split")
        first_rows_done = sem("first_rows_done")
        rows_added = sem("rows_added")
        rows_split = sem("rows_split")
        row_turned = sem("row_turned")
        shift_rows_ready = sem("shift_rows_ready")
        norm_shift_ready = sem("norm_shift_ready")
        vec = sem("vec")
        var_ready = sem("var_ready")
        std_ready = sem("std_ready")
        shift_ready = sem("shift_ready")
        out_ready = sem("out_ready")
        out_landed = sem("out_landed")

        N_CONSTS = 6
        CONSTS = 16 * N_CONSTS

        block = ctx.enter_context(nc.Block())

        def landed(eng, n, j, i, per):
            eng.wait_ge(raw_landed[(n + j) % RING], 16 * ((n + j) // RING + 1) + i * (16 * per // RING))

        @block.sync
        def _(sp):
            def load(slot, chunk):
                sp.dma_start(w_raw[:, slot, :], stream_d[chunk, :, :]).then_inc(raw_landed[slot], 16)

            def load_x(q):
                sp.dma_start(xt_raw[:, 4 * q:4 * q + 4, :], xt_d[q, :, :, :]).then_inc(x_landed[q], 16)

            def load_half(n, half):
                cols = slice(half * HALF * P, (half + 1) * HALF * P)
                sp.dma_start(w_raw[:, n, cols], stream_d[n, :, cols]).then_inc(
                    (first_half_landed[n], raw_landed[n])[half], 16)

            load_x(0)
            load_half(0, 0)
            load_x(1)
            load_half(0, 1)
            load_x(2)
            load_x(3)
            load_half(1, 0)
            load_half(1, 1)
            load(2, 2)
            for dst, src in ((ident[:, :], ident_d), (coef[:, :], coef_d), (gate_bias[:, :], bias_d),
                             (pool_scale[:, :], scale_d), (mask[:, :], mask_d), (inv[:, :, :], inv_d)):
                sp.dma_start(dst, src).then_inc(consts_landed, 16)
            whole = (CHUNKS - RING) // RING
            with sp.Fori(0, whole) as i:
                for j in range(RING):
                    sp.wait_ge(lo_split, i * (2 * RING) + 2 * (j + 1))
                    sp.dma_start(w_raw[:, j, :],
                                 stream_d[bass.ds(i * RING + (RING + j), 1), :, :]
                                 .rearrange("a p n -> (a p) n")).then_inc(raw_landed[j], 16)
            for n in range(RING * (whole + 1), CHUNKS):
                sp.wait_ge(lo_split, 2 * (n - RING + 1))
                load(n % RING, n)
            for n in range(TT * BLOCKS):
                sp.wait_ge(out_ready, n + 1)
                t, cols = n // BLOCKS, slice(n % BLOCKS * BLOCK, (n % BLOCKS + 1) * BLOCK)
                sp.dma_start(out_d[t, :, cols], res[:, t, cols]).then_inc(out_landed, 16)
            sp.wait_ge(out_landed, 16 * TT * BLOCKS)

        @block.tensor
        def _(pe):
            mm, turn = nc.tensor.matmul, nc.tensor.transpose

            ring_hi = w_hi[:, :, :].rearrange("p r c -> p (r c)")
            ring_lo = w_lo[:, :, :].rearrange("p r c -> p (r c)")

            def product(out, a_hi, a_lo, b_hi, b_lo, first=True, last=True):
                mm(out, a_hi, b_hi, start=first, stop=False)
                mm(out, a_hi, b_lo, start=False, stop=False)
                return mm(out, a_lo, b_hi, start=False, stop=last)

            def chunk(n, j, i, per, moving, between=None):
                slot = (n + j) % RING
                for half in range(2):
                    pe.wait_ge(lo_split, 2 * (n + j) + half + 1 + i * (2 * per))
                    for k in range(half * HALF, (half + 1) * HALF):
                        if between:
                            between(k)
                        bank, tile, first, last = moving(k)
                        cols = slice(k * P, (k + 1) * P)
                        mm(bank, w_hi[:, slot, cols], tile.rearrange("p a s -> p (a s)"),
                           start=first, stop=False)
                        done = mm(bank[:, SEQ:2 * SEQ], w_lo[:, slot, cols], tile[:, 0, :],
                                  start=False, stop=last)
                done.then_inc(chunk_done, 1)

            def next_bank(n, j, i):
                pe.wait_ge(proj_free, FROM + banked(n, j) + i * banked_per(n))

            def from_x(bank):
                return lambda k: (proj_ps[:, bank, :], xt[:, k, :, :], k == 0, k == KT - 1)

            def x_arrives(k):
                if k % 4 == 0:
                    pe.wait_ge(x_lo_done, k // 4 + 1)

            def scores(i):
                pe.wait_ge(qk_split, i * (2 * GROUPS) + 2 * GROUPS)
                pe.wait_ge(pt_split, FROM + i * GROUPS)
                q = slice(0, P)
                for g in range(GROUPS):
                    out = (attn_ps[:, 0:512] if g < 2 else attn_ps[:, THIRD:THIRD + 2 * P]).rearrange(
                        "p (a c) -> p a c", a=2)
                    cols = slice(g * P, (g + 1) * P) if g < 2 else q
                    mm(out[:, :, cols], q_hi[:, g, q], keys[:, g, :, 0:P], start=True, stop=False)
                    mm(out[:, 1, cols], q_lo[:, g, q], keys[:, g, 0, 0:P], start=False, stop=True)
                q = slice(P, SEQ)
                for g in range(GROUPS):
                    at = 512 + g * SEQ
                    done = product(attn_ps[:, at:at + SEQ], q_hi[:, g, q], q_lo[:, g, q],
                                   keys[:, g, 0, :], keys[:, g, 1, :])
                done.then_inc(scores_ready, 1)

            def turn_probs(i):
                pe.wait_ge(consts_landed, CONSTS)
                pe.wait_ge(probs_ready, i * 2 + 2)
                for g in range(GROUPS):
                    at = g * 512
                    turn(attn_ps[:, at:at + P], s_sb[:, g * P:(g + 1) * P], ident[:, :])
                    for kt in range(2):
                        src = S0 + g * SEQ + kt * P
                        done = turn(attn_ps[:, at + P + kt * P:at + 2 * P + kt * P],
                                    s_sb[:, src:src + P], ident[:, :])
                    done.then_inc(pt_ready, 1)

            def values(j, i):
                n = V_FIRST + j
                pe.wait_ge(lo_split, 2 * n + 2 + i * (2 * A_CHUNKS))
                if j == 0:
                    pe.wait_ge(v_split, FROM + i * TT)
                before, upto = j * KT // GROUPS, (j + 1) * KT // GROUPS
                for k in range(before, upto):
                    cols = slice(k * GROUPS * P, (k + 1) * GROUPS * P)
                    for t in range(TT):
                        tokens = slice(t * P, (t + 1) * P)
                        done = product(v_ps[t][:, :], xt[:, k, 0, tokens], xt[:, k, 1, tokens],
                                       ring_hi[:, cols], ring_lo[:, cols], k == 0, k == KT - 1)
                    if j > 0 and k == before:
                        done.then_inc(chunk_done, 1)
                if j == GROUPS - 1:
                    done.then_inc(chunk_done, 1)

            def mix(i):
                pe.wait_ge(pt_split, FROM + i * GROUPS + GROUPS)
                pe.wait_ge(v_split, FROM + i * TT + TT)
                pe.wait_ge(mixed_free, FROM + i)
                out = mixed_ps[:, :].rearrange("p (a q) -> p a q", a=2)
                for g in range(GROUPS):
                    v = slice(g * P, (g + 1) * P)
                    for kt in range(TT):
                        queries, cols = ((slice(0, SEQ), slice(0, SEQ)), (slice(P, SEQ), slice(SEQ, PTW)))[kt]
                        mm(out[:, :, queries], v_hi[:, kt, v], pt[:, g, :, cols],
                           start=(g == 0 and kt == 0), stop=False)
                        done = mm(out[:, 1, queries], v_lo[:, kt, v], pt[:, g, 0, cols],
                                  start=False, stop=(g == GROUPS - 1 and kt == TT - 1))
                done.then_inc(mixed_ready, 1)

            pe.wait_ge(zeros_ready, 1)
            for _ in range(WARM_UP):
                mm(mixed_ps[:, :], zeros[:, 0:P], zeros[:, :], start=True, stop=True)
            pe.sem_inc(chunk_done, FROM)
            with pe.Fori(0, A_STEPS) as i:
                for j in range(A_CHUNKS):
                    if V_FIRST <= j < V_FIRST + GROUPS:
                        values(j - V_FIRST, i)
                    else:
                        chunk(0, j, i, A_CHUNKS, from_x(j % 2), x_arrives if j == 0 else None)
                    next_bank(0, j, i)
                    if j == SCORES_AFTER:
                        scores(i)
                    if j == PT_AFTER:
                        turn_probs(i)
                mix(i)

            pe.wait_ge(lo_split, 2 * POOL_MAP + 2)
            pe.wait_ge(pool_split, POOL_TILES)
            slot = POOL_MAP % RING
            for g in range(POOL_TILES // 2):
                for m in range(2):
                    for kk in range(2):
                        cols = slice((g * 2 + kk) * POOL_GROUP + m * P, (g * 2 + kk) * POOL_GROUP + (m + 1) * P)
                        last = product(attn_ps[:, g * 512 + m * SEQ:g * 512 + (m + 1) * SEQ],
                                       w_hi[:, slot, cols], w_lo[:, slot, cols],
                                       p_hi[:, 2 * g + kk, :], p_lo[:, 2 * g + kk, :],
                                       first=(kk == 0), last=(kk == 1))
                last.then_inc(pool_ready if g < POOL_TILES // 2 - 1 else chunk_done, 1)
            next_bank(B_FIRST, 0, 0)

            def from_y(k):
                bank, kk = k // HALF, k % HALF
                return (attn_ps[:, bank * 512:(bank + 1) * 512], (ya, yp)[bank][:, kk, :, :],
                        kk == 0, kk == HALF - 1)

            with pe.Fori(0, B_STEPS) as i:
                for j in range(B_CHUNKS):
                    bank = (B_FIRST + j) % 2
                    if j % 3 < 2:
                        chunk(B_FIRST, j, i, B_CHUNKS, from_x(bank))
                    else:
                        pe.wait_ge(y_split, HEADS)
                        pe.wait_ge(yp_split, POOL_TILES // 2)
                        chunk(B_FIRST, j, i, B_CHUNKS, from_y)
                    next_bank(B_FIRST, j, i)

            def out_products(n, kk, t):
                c, k = (n - C_FIRST) // BLOCK_CHUNKS, (n - C_FIRST) % BLOCK_CHUNKS * BLOCK_KT + kk
                cols, tokens = slice(kk * BLOCK, (kk + 1) * BLOCK), slice(t * P, (t + 1) * P)
                if k == 0 and c >= 2:
                    pe.wait_ge(rows_added, TT * (c - 2) + t + 1)
                return product(block_sum(c, t)[:, :], merged[:, k, 0, tokens], merged[:, k, 1, tokens],
                               w_hi[:, n % RING, cols], w_lo[:, n % RING, cols], k == 0, k == KT - 1)

            pe.wait_ge(merged_split, OT - 1)
            for n in range(C_FIRST, CHUNKS - 1):
                if n == C_FIRST + BLOCK_CHUNKS - 1:
                    pe.wait_ge(merged_split, OT)
                for kk in range(BLOCK_KT):
                    if kk % 2 == 0:
                        pe.wait_ge(lo_split, 2 * n + kk // 2 + 1)
                    for t in range(TT):
                        done = out_products(n, kk, t)
                done.then_inc(chunk_done, 1)
            pe.wait_ge(lo_split, 2 * CHUNKS)
            for t in range(TT):
                for kk in range(BLOCK_KT):
                    done = out_products(CHUNKS - 1, kk, t)
                done.then_inc((first_rows_done, chunk_done)[t], 1)

            def turn_row(t):
                pe.wait_ge(shift_ready, t + 1)
                turn((value_ps, mixed_ps)[t][0:ROWS, 0:P], shift_parts[:, t, 0:ROWS],
                     ident[:, :]).then_inc(row_turned, 1)

            def shift_product(t, c):
                mm(norm_shift(t, c)[:, :], shift_rows[0:ROWS, t, :], row_parts[0:ROWS, c * BLOCK:(c + 1) * BLOCK],
                   start=True, stop=True).then_inc(norm_shift_ready, 1)

            turn_row(0)
            pe.wait_ge(rows_split, 1)
            pe.wait_ge(shift_rows_ready, 1)
            for c in range(BLOCKS):
                shift_product(0, c)
            turn_row(1)
            pe.wait_ge(shift_rows_ready, 2)
            pe.wait_ge(rows_added, TT * BLOCKS)
            for c in range(BLOCKS):
                shift_product(1, c)

        @block.scalar
        def _(act):
            activation = nc.scalar.activation

            def hi_part(slot, half):
                cols = slice(half * HALF * P, (half + 1) * HALF * P)
                activation(w_hi[:, slot, cols], w_raw[:, slot, cols], ACT.Copy).then_inc(hi_split, 1)

            def split_hi(n, j, i, per):
                landed(act, n, j, i, per)
                if n or j >= RING or per:
                    act.wait_ge(chunk_done, FROM + n + j - AHEAD + i * per)
                for half in range(2):
                    hi_part((n + j) % RING, half)

            def correction(n, j, i, per, pair=False):
                act.wait_ge(chunk_done, FROM + n + j + 1 + i * per)
                if pair:
                    act.wait_ge(proj_free, FROM + banked(n, j) - 2 + i * banked_per(n))
                    activation(corr_pair[:, :, :], proj_pair[:, :, SEQ:2 * SEQ], ACT.Copy).then_inc(act_evac, 1)
                else:
                    b = (n + j) % 2
                    activation(corr[:, b, :], proj_ps[:, b, SEQ:2 * SEQ], ACT.Copy).then_inc(act_evac, 1)
                act.wait_ge(proj_free, FROM + banked(n, j) + i * banked_per(n))

            for q in range(4):
                act.wait_ge(x_landed[q], 16)
                activation(xt[:, 4 * q:4 * q + 4, 0, :], xt_raw[:, 4 * q:4 * q + 4, :],
                           ACT.Copy).then_inc(x_hi_done, 1)
                if q < 2:
                    act.wait_ge((first_half_landed[0], raw_landed[0])[q], 16)
                    hi_part(0, q)
            for half in range(2):
                act.wait_ge((first_half_landed[1], raw_landed[1])[half], 16)
                hi_part(1, half)

            def exp_probs(i):
                act.wait_ge(max_ready, i + 1)
                for t, cols in ((0, slice(0, S0)), (1, slice(S0, S0 + S1))):
                    activation(s_sb[:, cols], s_sb[:, cols], ACT.Exp, bias=nmax[:, t:t + 1], scale=SCALE,
                               accum_out=den[:, t:t + 1]).then_inc(exp_done, 1)

            def v_hi_parts(i):
                act.wait_ge(chunk_done, FROM + V_FIRST + GROUPS + i * A_CHUNKS)
                for t in range(TT):
                    activation(v_hi[:, t, :], v_ps[t][:, :], ACT.Copy).then_inc(v_hi_done, 1)

            with act.Fori(0, A_STEPS) as i:
                for j in range(A_CHUNKS):
                    if j == SOFTMAX_SUM:
                        exp_probs(i)
                    if j == PT_SPLIT:
                        for g in range(GROUPS):
                            act.wait_ge(pt_ready, i * GROUPS + g + 1)
                            activation(pt[:, g, 0, :], attn_ps[:, g * 512:g * 512 + PTW],
                                       ACT.Copy).then_inc(pt_hi_done, 1)
                    split_hi(0, j + AHEAD, i, A_CHUNKS)
                    if j == V_FIRST + GROUPS - 1:
                        v_hi_parts(i)
                    if j == Z_ATTN:
                        act.wait_ge(proj_free, FROM + banked(0, j) + i * A_BANKED)
                    if not V_FIRST <= j < V_FIRST + GROUPS:
                        correction(0, j, i, A_CHUNKS)
                    if j in (Z_ATTN, Z_POOL):
                        act.wait_ge(proj_free, FROM + banked(0, j) + 1 + i * A_BANKED)
                        z = int(j == Z_POOL)
                        activation(th_gate[:, z, :], gate_f[:, z, :], ACT.Tanh, scale=0.5).then_inc(tanh_done, 1)

                act.wait_ge(mixed_ready, i + 1)
                activation(mixed_corr[:, :], mixed_ps[:, SEQ:2 * SEQ], ACT.Copy).then_inc(mixed_corr_done, 1)

            split_hi(POOL_MAP, AHEAD, 0, 0)
            act.wait_ge(chunk_done, FROM + POOL_MAP + 1)
            act.dma_start(res[:, :, :], x_d).then_inc(tail_landed, 16)
            for g in range(POOL_TILES // 2):
                act.wait_ge(yp_f_ready, g + 1)
                activation(yp[:, 2 * g:2 * g + 2, 0, :],
                           yp_f[:, g % 2, :].rearrange("p (m s) -> p m s", m=2), ACT.Copy).then_inc(yp_hi_done, 1)
            act.wait_ge(bias_ready, 1)
            with act.Fori(0, B_STEPS) as i:
                for j in range(B_CHUNKS):
                    split_hi(B_FIRST, j + AHEAD, i, B_CHUNKS)
                    correction(B_FIRST, j, i, B_CHUNKS, pair=j % 3 == 2)
                    if j % 3 < 2:
                        act.wait_ge(proj_free, FROM + banked(B_FIRST, j) + 1 + i * B_CHUNKS)
                        activation(th_gate[:, j % 3, :], gate_f[:, j % 3, :], ACT.Tanh,
                                   bias=half_bias[:, bass.ds(i * 4 + ((j % 3) * OT + j // 3), 1)],
                                   scale=0.5).then_inc(tanh_done, 1)
            act.wait_ge(chunk_done, FROM + C_FIRST)
            act.dma_start(gamma[:, :], gamma_d).then_inc(tail_landed, 16)
            act.dma_start(rows[0:ROWS, :], rows_d).then_inc(tail_landed, 16)
            act.dma_start(row_kind[0:ROWS, 0:2], row_kind_d).then_inc(tail_landed, 16)
            whole = (OT - AHEAD) // RING
            with act.Fori(0, whole) as i:
                for j in range(RING):
                    split_hi(C_FIRST, j + AHEAD, i, RING)
            for e in range(whole * RING + AHEAD, OT):
                split_hi(C_FIRST, e, 0, 0)
            activation(rstd[:, 4:5], ident[:, 0:1], ACT.Sqrt)
            for t in range(TT):
                act.wait_ge(var_ready, t + 1)
                activation(rstd[:, t:t + 1], mv[:, t, 2:3], ACT.Sqrt).then_inc(std_ready, 1)
                act.wait_ge(row_turned, t + 1)
                activation(shift_rows[0:ROWS, t, :], (value_ps, mixed_ps)[t][0:ROWS, 0:P],
                           ACT.Copy).then_inc(shift_rows_ready, 1)

        @block.vector
        def _(dve):
            tt, ts = nc.vector.tensor_tensor, nc.vector.tensor_scalar
            stt, copy = nc.vector.scalar_tensor_tensor, nc.vector.tensor_copy

            class Chain:
                count, per, i = 0, 0, 0

                def ready(self):
                    dve.wait_ge(vec, self.count + (self.i * self.per if self.per else 0))

                def add(self, ins):
                    ins.then_inc(vec, 1)
                    self.count += 1

                def link(self, ins):
                    self.add(ins)
                    self.ready()

            chain = Chain()
            for counted in (proj_free, pt_split, v_split, mixed_free):
                dve.sem_inc(counted, FROM)

            def lo_part(slot, half):
                cols = slice(half * HALF * P, (half + 1) * HALF * P)
                tt(w_lo[:, slot, cols], w_raw[:, slot, cols], w_hi[:, slot, cols].bitcast(F32),
                   ALU.subtract).then_inc(lo_split, 1)

            def split_lo(n, j, i, per):
                slot = (n + j) % RING
                for half in range(2):
                    dve.wait_ge(hi_split, 2 * (n + j) + half + 1 + i * (2 * per))
                    lo_part(slot, half)

            def halves_summed(dst, n, j, i):
                dve.wait_ge(act_evac, banked(n, j) + 1 + i * banked_per(n))
                tt(dst, proj_ps[:, (n + j) % 2, 0:SEQ], corr[:, (n + j) % 2, :], ALU.add).then_inc(proj_free, 1)

            def freed(n, j, i):
                dve.wait_ge(proj_free, FROM + banked(n, j) + 1 + i * banked_per(n))

            nc.vector.memset(zeros[:, :].bitcast(F32), 0.0).then_inc(zeros_ready, 1)
            for q in range(4):
                dve.wait_ge(x_hi_done, q + 1)
                tt(xt[:, 4 * q:4 * q + 4, 1, :], xt_raw[:, 4 * q:4 * q + 4, :],
                   xt[:, 4 * q:4 * q + 4, 0, :].bitcast(F32), ALU.subtract).then_inc(x_lo_done, 1)
                if q < 2:
                    dve.wait_ge(hi_split, q + 1)
                    lo_part(0, q)
            split_lo(0, 1, 0, 0)
            for pad in (u_pad, pool_a, pool_b):
                chain.add(nc.vector.memset(pad[:, 0:PAD], 0.0))
            chain.ready()

            def sigmoid(z, count, i, per):
                dve.wait_ge(tanh_done, count + i * per)
                chain.link(ts(gate[:, z, :], th_gate[:, z, :], 0.5, 0.5, ALU.mult, ALU.add))

            def masked_max(i):
                dve.wait_ge(scores_ready, i + 1)
                dve.wait_ge(consts_landed, CONSTS)
                chain.add(tt(s_sb[:, 0:2 * P], attn_ps[:, 2 * P:4 * P], mask[:, 0:2 * P], ALU.add))
                chain.link(tt(s_sb[:, 2 * P:S0], attn_ps[:, THIRD + P:THIRD + 2 * P], mask[:, 2 * P:S0], ALU.add))
                chain.add(nc.vector.memset(smax[:, 4:6], 0.0))
                for n, at, cols, rest in ((0, 0, slice(0, 2 * P), s_sb), (2, THIRD, slice(2 * P, S0), s_sb),
                                          (1, 512, slice(S0, S0 + S1), mask)):
                    chain.add(nc.vector.tensor_tensor_reduce(
                        s_sb[:, cols], attn_ps[:, at:at + cols.stop - cols.start], rest[:, cols], 1.0,
                        -3.0e38, ALU.add, ALU.max, smax[:, n:n + 1]))
                chain.ready()
                chain.link(tt(smax[:, 0:1], smax[:, 0:1], smax[:, 2:3], ALU.max))
                ts(nmax[:, 0:2], smax[:, 0:2], -SCALE, None, ALU.mult).then_inc(max_ready, 1)

            def normalise(i):
                dve.wait_ge(exp_done, i * 2 + 2)
                chain.link(nc.vector.reciprocal(rden[:, 0:2], den[:, 0:2]))
                for t, cols in ((0, slice(0, S0)), (1, slice(S0, S0 + S1))):
                    ts(s_sb[:, cols], s_sb[:, cols], rden[:, t:t + 1], None, ALU.mult).then_inc(probs_ready, 1)

            def pool(h):
                src = u_pad
                for k, dst in enumerate((pool_a, pool_b, pool_a, pool_b)):
                    back = PAD - 2 ** k
                    chain.link(stt(out=dst[:, PAD:PAD + SEQ], in0=src[:, back:back + SEQ],
                                   scalar=coef[:, bass.ds(h * POOL_COEFS + k, 1)],
                                   in1=src[:, PAD:PAD + SEQ], op0=ALU.mult, op1=ALU.add))
                    src = dst
                chain.link(tt(pool_a[:, PAD:2 * PAD], src[:, PAD:2 * PAD], tile_of(inv, h), ALU.mult))
                chain.add(tt(sum_f[:, 0:PAD], pool_a[:, PAD:2 * PAD], u_pad[:, PAD:2 * PAD], ALU.subtract))
                chain.link(stt(out=sum_f[:, PAD:SEQ], in0=src[:, 2 * PAD:PAD + SEQ],
                               scalar=coef[:, bass.ds(h * POOL_COEFS + POOL_STEPS, 1)],
                               in1=u_pad[:, 2 * PAD:PAD + SEQ], op0=ALU.mult, op1=ALU.subtract))
                chain.link(copy(tile_of(p_hi, h), sum_f[:, :]))
                tt(tile_of(p_lo, h), sum_f[:, :], tile_of(p_hi, h).bitcast(F32), ALU.subtract).then_inc(pool_split, 1)

            def tile_of(t, tile):
                return t[:, bass.ds(tile, 1), :].rearrange("p a s -> p (a s)")

            def split(src, parts, tile, signal):
                both = parts[:, bass.ds(tile, 1), :, :].rearrange("p a b s -> p (a b) s")
                chain.link(copy(both[:, 0, :], src))
                tt(both[:, 1, :], src, both[:, 0, :].bitcast(F32), ALU.subtract).then_inc(signal, 1)

            per_a = 28
            start_a = chain.count
            with dve.Fori(0, A_STEPS) as i:
                chain.i, chain.per = i, per_a
                for j in range(A_CHUNKS):
                    if j == SOFTMAX_SUM:
                        normalise(i)
                    if j == PT_SPLIT:
                        for g in range(GROUPS):
                            dve.wait_ge(pt_hi_done, i * GROUPS + g + 1)
                            tt(pt[:, g, 1, :], attn_ps[:, g * 512:g * 512 + PTW],
                               pt[:, g, 0, :].bitcast(F32), ALU.subtract).then_inc(pt_split, 1)
                    if j == Z_POOL:
                        freed(0, U_POOL, i)
                        pool(i)
                    split_lo(0, j + AHEAD, i, A_CHUNKS)
                    if j < V_FIRST:
                        g = j // 2
                        hi, lo = ((q_hi[:, g, :], q_lo[:, g, :]), (keys[:, g, 0, :], keys[:, g, 1, :]))[j % 2]
                        halves_summed(qk_f[:, j % 2, :], 0, j, i)
                        freed(0, j, i)
                        chain.link(copy(hi, qk_f[:, j % 2, :]))
                        tt(lo, qk_f[:, j % 2, :], hi.bitcast(F32),
                           ALU.subtract).then_inc(qk_split, 1)
                    if j == SCORES_AFTER:
                        masked_max(i)
                    if j == Z_ATTN:
                        halves_summed(gate_f[:, 0, :], 0, j, i)
                        sigmoid(0, 1, i, 2)
                        chain.add(tt(silu_za[:, :], gate_f[:, 0, :], gate[:, 0, :], ALU.mult))
                    if j == V_FIRST + GROUPS - 1:
                        for t in range(TT):
                            dve.wait_ge(v_hi_done, i * TT + t + 1)
                            tt(v_lo[:, t, :], v_ps[t][:, :], v_hi[:, t, :].bitcast(F32),
                               ALU.subtract).then_inc(v_split, 1)
                    if j == U_POOL:
                        halves_summed(u_pad[:, PAD:PAD + SEQ], 0, j, i)
                    if j == Z_POOL:
                        halves_summed(gate_f[:, 1, :], 0, j, i)
                        sigmoid(1, 2, i, 2)
                        chain.add(stt(out=tile_of(szp, i), in0=gate_f[:, 1, :],
                                      scalar=pool_scale[:, bass.ds(i, 1)], in1=gate[:, 1, :],
                                      op0=ALU.mult, op1=ALU.mult))
                dve.wait_ge(mixed_corr_done, i + 1)
                tt(mixed_f[:, :], mixed_ps[:, 0:SEQ], mixed_corr[:, :], ALU.add).then_inc(mixed_free, 1)
                dve.wait_ge(mixed_free, FROM + i + 1)
                chain.link(tt(mixed_f[:, :], mixed_f[:, :], silu_za[:, :], ALU.mult))
                split(mixed_f[:, :], ya, i, y_split)
            assert chain.count - start_a == per_a, chain.count - start_a
            chain.count, chain.per = start_a + per_a * A_STEPS, 0

            split_lo(POOL_MAP, AHEAD, 0, 0)
            ts(half_bias[:, :], gate_bias[:, :], 0.5, None, ALU.mult).then_inc(bias_ready, 1)
            for g in range(POOL_TILES // 2):
                if g < POOL_TILES // 2 - 1:
                    dve.wait_ge(pool_ready, g + 1)
                else:
                    dve.wait_ge(chunk_done, FROM + POOL_MAP + 1)
                if g >= 2:
                    dve.wait_ge(yp_split, g - 1)
                tt(yp_f[:, g % 2, :], attn_ps[:, g * 512:(g + 1) * 512],
                   szp[:, 2 * g:2 * g + 2, :].rearrange("p a s -> p (a s)"), ALU.mult).then_inc(yp_f_ready, 1)
                if g % 2 == 1:
                    for b in (g - 1, g):
                        dve.wait_ge(yp_hi_done, b + 1)
                        tt(yp[:, 2 * b:2 * b + 2, 1, :], yp_f[:, b % 2, :].rearrange("p (m s) -> p m s", m=2),
                           yp[:, 2 * b:2 * b + 2, 0, :].bitcast(F32), ALU.subtract).then_inc(yp_split, 1)

            per_b = 4 * 5
            start_b = chain.count
            with dve.Fori(0, B_STEPS) as i:
                chain.i, chain.per = i, per_b
                for j in range(B_CHUNKS):
                    split_lo(B_FIRST, j + AHEAD, i, B_CHUNKS)
                    tanhs = 2 * A_STEPS + j // 3 * 2
                    if j % 3 < 2:
                        if j % 3 == 1:
                            sigmoid(0, tanhs + 1, i, 2 * B_STEPS)
                        halves_summed(gate_f[:, j % 3, :], B_FIRST, j, i)
                    else:
                        sigmoid(1, tanhs + 2, i, 2 * B_STEPS)
                        dve.wait_ge(act_evac, banked(B_FIRST, j) + 1 + i * B_CHUNKS)
                        tt(pair_f[:, :, :], proj_pair[:, :, 0:SEQ], corr_pair[:, :, :],
                           ALU.add).then_inc(proj_free, 1)
                        freed(B_FIRST, j, i)
                        chain.link(tt(pair_f[:, :, :], pair_f[:, :, :], gate[:, :, :], ALU.mult))
                        chain.link(tt(sum_f[:, :], pair_f[:, 0, :], pair_f[:, 1, :], ALU.add))
                        split(sum_f[:, :], merged, i * 4 + j // 3, merged_split)
            assert chain.count - start_b == per_b, chain.count - start_b
            chain.count, chain.per = start_b + per_b * B_STEPS, 0

            def add_rows(c, t):
                at = res[:, t, c * BLOCK:(c + 1) * BLOCK]
                stt(out=at, in0=at, scalar=ALPHA, in1=block_sum(c, t)[:, :],
                    op0=ALU.mult, op1=ALU.add).then_inc(rows_added, 1)

            def statistics(c, t):
                dve.wait_ge(rows_added, TT * c + t + 1)
                chain.add(nc.vector.bn_stats(stats[:, t, c, :], res[:, t, c * BLOCK:(c + 1) * BLOCK]))

            def times_gamma(c, t):
                at = res[:, t, c * BLOCK:(c + 1) * BLOCK]
                chain.add(tt(at, at, gamma[:, c * BLOCK:(c + 1) * BLOCK], ALU.mult))

            def variance(t):
                chain.ready()
                chain.link(nc.vector.bn_aggr(mv[:, t, 0:2], stats[:, t, :, :].rearrange("p a s -> p (a s)")))
                ts(mv[:, t, 2:3], mv[:, t, 1:2], LN_EPS, None, ALU.add).then_inc(var_ready, 1)

            def token_rstd(t):
                dve.wait_ge(std_ready, t + 1)
                chain.add(nc.vector.reciprocal(rstd[:, 2 + t:3 + t], rstd[:, t:t + 1]))

            def token_shift(t):
                chain.ready()
                for out in (shift[:, t:t + 1], shift_parts[:, t, 0:1].bitcast(F32R),
                            shift_parts[:, t, 1:2].bitcast(F32R)):
                    chain.add(stt(out=out, in0=mv[:, t, 0:1], scalar=-1.0, in1=rstd[:, 2 + t:3 + t],
                                  op0=ALU.mult, op1=ALU.mult))

            def token_shift_lo(t):
                chain.ready()
                tt(shift_parts[:, t, 2:3].bitcast(F32R), shift[:, t:t + 1], shift_parts[:, t, 0:1],
                   ALU.subtract).then_inc(shift_ready, 1)

            def normalise_rows(t, c):
                dve.wait_ge(norm_shift_ready, t * BLOCKS + c + 1)
                at = res[:, t, c * BLOCK:(c + 1) * BLOCK]
                stt(out=at, in0=at, scalar=rstd[:, 2 + t:3 + t], in1=norm_shift(t, c)[:, :],
                    op0=ALU.mult, op1=ALU.add).then_inc(out_ready, 1)

            chain.link(nc.vector.memset(shift_parts[:, :, :], 1.0))
            for e in range(OT - 1):
                if e + AHEAD < OT:
                    split_lo(C_FIRST, e + AHEAD, 0, 0)
                if e % BLOCK_CHUNKS == BLOCK_CHUNKS - 1:
                    c = e // BLOCK_CHUNKS
                    dve.wait_ge(chunk_done, FROM + C_FIRST + e + 1)
                    dve.wait_ge(tail_landed, 16 * 4)
                    for t in range(TT):
                        add_rows(c, t)
                    for t in range(TT):
                        statistics(c, t)
                    chain.ready()
                    for t in range(TT):
                        times_gamma(c, t)
            chain.link(copy(rows_hi[0:ROWS, :].bitcast(F32R), rows[0:ROWS, :]))
            chain.link(ts(rows_signed[0:ROWS, :], rows_hi[0:ROWS, :], row_kind[0:ROWS, 1:2], None, ALU.mult))
            stt(out=row_parts[0:ROWS, :], in0=rows[0:ROWS, :], scalar=row_kind[0:ROWS, 0:1],
                in1=rows_signed[0:ROWS, :], op0=ALU.mult, op1=ALU.add).then_inc(rows_split, 1)
            c = BLOCKS - 1
            dve.wait_ge(first_rows_done, 1)
            add_rows(c, 0)
            statistics(c, 0)
            variance(0)
            times_gamma(c, 0)
            token_rstd(0)
            token_shift(0)
            token_shift_lo(0)
            dve.wait_ge(chunk_done, FROM + CHUNKS)
            add_rows(c, 1)
            statistics(c, 1)
            variance(1)
            normalise_rows(0, 0)
            token_rstd(1)
            times_gamma(c, 1)
            token_shift(1)
            token_shift_lo(1)
            for b in range(1, BLOCKS):
                normalise_rows(0, b)
            for b in range(BLOCKS):
                normalise_rows(1, b)


def _mask():
    t, s = np.arange(SEQ)[:, None], np.arange(SEQ)[None, :]
    tiles = []
    for tile in range(TT):
        for window, dilation in DILATED:
            sees = (s <= t) & (t - s <= window) & ((t - s) % dilation == 0)
            m = np.where(sees, 0.0, NEG_INF).astype(np.float32)
            tiles.append(m[tile * P:(tile + 1) * P, :(tile + 1) * P])
    return np.ascontiguousarray(np.concatenate(tiles, axis=1))


def _pool_tables():
    coef = np.zeros((POOL_TILES, POOL_COEFS), np.float32)
    inv = np.zeros((POOL_TILES, PAD), np.float32)
    for tile in range(POOL_TILES):
        w = POOL_WINDOWS[tile * P // POOL_GROUP]
        coef[tile, :int(np.log2(w))] = 1.0
        coef[tile, POOL_STEPS] = 1.0 / w
        inv[tile] = 1.0 / np.minimum(np.arange(1, PAD + 1), w).astype(np.float32)
    return (np.ascontiguousarray(np.broadcast_to(coef.reshape(1, -1), (P, POOL_TILES * POOL_COEFS))),
            np.ascontiguousarray(np.broadcast_to(inv.reshape(1, POOL_TILES, PAD), (P, POOL_TILES, PAD))))


def _tiles(w):
    k, n = w.shape
    return w.reshape(k // P, P, n // P, P).transpose(2, 1, 0, 3)


def _stream(w_in, w_pool, w_proj_attn, w_proj_pool, w_out):
    cols = _tiles(w_in)
    qkv = GROUPS * HEADS
    z_attn, u_pool, z_pool = 3 * qkv, 3 * qkv + HEADS, 3 * qkv + HEADS + POOL_TILES
    gates = z_pool + POOL_TILES
    stream = np.empty((CHUNKS, P, CHUNK), np.float32)
    n = 0
    for h in range(HEADS):
        order = [part * qkv + g * HEADS + h for g in range(GROUPS) for part in range(2)]
        order += [None] * GROUPS + [z_attn + h, u_pool + h, z_pool + h]
        for j, tile in enumerate(order):
            if tile is not None:
                stream[n + j] = cols[tile].reshape(P, CHUNK)
        values = cols[2 * qkv + h:3 * qkv:HEADS].transpose(1, 2, 0, 3).reshape(P, GROUPS, CHUNK)
        stream[n + V_FIRST:n + V_FIRST + GROUPS] = values.transpose(1, 0, 2)
        n += A_CHUNKS
    stream[n] = w_pool.reshape(4, 2, P, POOL_GROUP).transpose(2, 0, 1, 3).reshape(P, CHUNK)
    n += 1
    attn, pool = _tiles(w_proj_attn), _tiles(w_proj_pool)
    last = w_out.reshape(BLOCK_CHUNKS, BLOCK_KT, P, BLOCKS, BLOCK).transpose(3, 0, 2, 1, 4)
    for d in range(OT):
        stream[n] = cols[gates + d].reshape(P, CHUNK)
        stream[n + 1] = cols[gates + OT + d].reshape(P, CHUNK)
        stream[n + 2] = np.concatenate([attn[d], pool[d]], axis=1).reshape(P, CHUNK)
        n += 3
    stream[n:] = last.reshape(OT, P, CHUNK)
    return stream


def kernel(x, w_in, b_gate, w_pool, pool_scale, w_proj_attn, w_proj_pool, w_out, ln_gamma, ln_beta):
    import concourse.bacc as bacc
    from concourse.bass_utils import run_bass_kernel_spmd

    x = np.asarray(x)[0]
    w_in, b_gate, w_pool, pool_scale, w_proj_attn, w_proj_pool, w_out, ln_gamma, ln_beta = (
        np.asarray(a)[0] for a in (w_in, b_gate, w_pool, pool_scale, w_proj_attn, w_proj_pool, w_out,
                                   ln_gamma, ln_beta))
    coef, inv = _pool_tables()
    arrays = {
        "xt": x.T.reshape(4, 4, P, SEQ).transpose(0, 2, 1, 3),
        "x_rows": x.reshape(TT, P, D_MODEL).transpose(1, 0, 2),
        "weights": _stream(w_in, w_pool, w_proj_attn, w_proj_pool, w_out),
        "gate_bias": b_gate.reshape(2 * OT, P).T,
        "pool_scale": pool_scale.reshape(POOL_TILES, P).T,
        "gamma_row": ln_gamma.reshape(1, D_MODEL).repeat(P, axis=0),
        "rows": np.stack([ln_gamma, ln_gamma, ln_gamma, ln_beta, ln_beta]),
        "row_kind": np.array([(0, 1), (1, -1), (0, 1), (0, 1), (1, -1)], np.float32),
        "identity": np.eye(P, dtype=np.float32),
        "mask": _mask(),
        "pool_coef": coef,
        "pool_inv": inv,
    }
    arrays = {f"in_{k}": np.ascontiguousarray(v) for k, v in arrays.items()}
    nc = bacc.Bacc("TRN2", target_bir_lowering=False, num_devices=1)
    args = [nc.dram_tensor(k, v.shape, mybir.dt.from_np(v.dtype), kind="ExternalInput").ap()
            for k, v in arrays.items()]
    args.append(nc.dram_tensor("out_rows", (TT, P, D_MODEL), F32, kind="ExternalOutput").ap())
    layer_kernel(nc, *args)
    r = run_bass_kernel_spmd(nc, [arrays], core_ids=[0])
    return r.results[0]["out_rows"].reshape(1, SEQ, D_MODEL)
```
